# Optimizing a Trainium2 kernel written in Bass

```python
import math
import jax, jax.numpy as jnp
from jax import lax
import numpy as np

D_MODEL = 1024
BATCH = 1
SEQ = 1024
DEPTH = 1
DEC_BATCH = 8
DEC_SEQ = 1
PAST_LEN = 8192
PAGE_SIZE = 128

H_MLSTM = 4
DK_MLSTM = D_MODEL // 8
DV_MLSTM = D_MODEL // 8
W_MLSTM = H_MLSTM * DV_MLSTM
H_RET = 4
DK_RET = D_MODEL // 8
DV_RET = D_MODEL // 8
W_RET = H_RET * DV_RET
MIX_WIDTH = W_MLSTM + W_RET
CHUNK = 128
ROPE_BASE = 10000.0
EPS = 1e-6
PEER_HEADS = 8
PEER_NKEYS = 128
PEER_EXPERTS = PEER_NKEYS * PEER_NKEYS
PEER_QDIM = 256
PEER_HALF = PEER_QDIM // 2
PEER_TOPK = 16
PEER_BLOCK = 128

OFF_MQ = 0
OFF_MK = OFF_MQ + H_MLSTM * DK_MLSTM
OFF_MV = OFF_MK + H_MLSTM * DK_MLSTM
OFF_MO = OFF_MV + W_MLSTM
OFF_MI = OFF_MO + W_MLSTM
OFF_MF = OFF_MI + H_MLSTM
OFF_RQ = OFF_MF + H_MLSTM
OFF_RK = OFF_RQ + H_RET * DK_RET
OFF_RV = OFF_RK + H_RET * DK_RET
OFF_RG = OFF_RV + W_RET
PROJ_WIDTH = OFF_RG + W_RET

kernel_name = 'hymba_mlstm_retention_peer_step'

def rmsnorm(x, g):
    xf = x.astype(jnp.float32)
    y = xf * lax.rsqrt(jnp.mean(xf * xf, axis=-1, keepdims=True) + EPS)
    return (y * g.astype(jnp.float32)).astype(x.dtype)

def head_norm(h, g, n_heads):
    B, L, W = h.shape
    hh = h.reshape(B, L, n_heads, W // n_heads)
    mu = jnp.mean(hh, axis=-1, keepdims=True)
    var = jnp.mean(jnp.square(hh - mu), axis=-1, keepdims=True)
    hh = (hh - mu) * lax.rsqrt(var + EPS)
    return hh.reshape(B, L, W) * g.astype(jnp.float32)

def rotary(t, pos):
    d = t.shape[-1]
    half = d // 2
    inv = jnp.power(ROPE_BASE, -jnp.arange(half, dtype=jnp.float32) * (2.0 / d))
    ang = pos[:, None, :, None].astype(jnp.float32) * inv
    c, s = jnp.cos(ang), jnp.sin(ang)
    t1, t2 = t[..., :half], t[..., half:]
    return jnp.concatenate([t1 * c - t2 * s, t1 * s + t2 * c], axis=-1)

def to_chunks(t, c):
    B, H, L = t.shape[:3]
    return jnp.moveaxis(t.reshape(B, H, L // c, c, *t.shape[3:]), 2, 0)

def from_chunks(t):
    nC, B, H, c = t.shape[:4]
    return jnp.moveaxis(t, 0, 2).reshape(B, H, nC * c, *t.shape[4:])

def mlstm_chunkwise(q, k, v, ig, lf, C0, n0, m0, c):
    causal = jnp.tril(jnp.ones((c, c), dtype=bool))

    def step(carry, inp):
        C, n, m = carry
        qc, kc, vc, ic, fc = inp
        b = jnp.cumsum(fc, axis=-1)
        d_intra = jnp.where(causal, b[..., :, None] - b[..., None, :] + ic[..., None, :], -jnp.inf)
        d_inter = b + m[..., None]
        m_t = jnp.maximum(d_inter, jnp.max(d_intra, axis=-1))
        w_inter = jnp.exp(d_inter - m_t)
        s = jnp.einsum('bhtd,bhjd->bhtj', qc, kc) * jnp.exp(d_intra - m_t[..., None])
        num = w_inter[..., None] * jnp.einsum('bhtd,bhde->bhte', qc, C) + jnp.einsum('bhtj,bhje->bhte', s, vc)
        den = w_inter * jnp.einsum('bhtd,bhd->bht', qc, n) + jnp.sum(s, axis=-1)
        h = num / jnp.maximum(jnp.abs(den), jnp.exp(-m_t))[..., None]
        b_last = b[..., -1]
        m_new = m_t[..., -1]
        a = jnp.exp(b_last[..., None] - b + ic - m_new[..., None])
        decay = jnp.exp(b_last + m - m_new)
        ka = kc * a[..., None]
        C = decay[..., None, None] * C + jnp.einsum('bhjd,bhje->bhde', ka, vc)
        n = decay[..., None] * n + jnp.sum(ka, axis=2)
        return (C, n, m_new), h

    (C, n, m), h = lax.scan(step, (C0, n0, m0),
                            (to_chunks(q, c), to_chunks(k, c), to_chunks(v, c), to_chunks(ig, c), to_chunks(lf, c)))
    return from_chunks(h), C, n, m

def retention_chunkwise(q, k, v, S0, c):
    H = q.shape[1]
    lg = jnp.log1p(-jnp.power(2.0, -5.0 - jnp.arange(H, dtype=jnp.float32)))
    idx = jnp.arange(c, dtype=jnp.float32)
    diff = idx[:, None] - idx[None, :]
    dmat = jnp.where(diff >= 0, jnp.exp(jnp.maximum(diff, 0.0) * lg[:, None, None]), 0.0)
    q_dec = jnp.exp((idx + 1.0) * lg[:, None])[..., None]
    k_dec = jnp.exp((c - 1.0 - idx) * lg[:, None])[..., None]
    chunk_dec = jnp.exp(c * lg)[:, None, None]

    def step(S, inp):
        qc, kc, vc = inp
        inner = jnp.einsum('bhtj,bhje->bhte', jnp.einsum('bhtd,bhjd->bhtj', qc, kc) * dmat, vc)
        cross = jnp.einsum('bhtd,bhde->bhte', qc, S) * q_dec
        S = chunk_dec * S + jnp.einsum('bhjd,bhje->bhde', kc * k_dec, vc)
        return S, inner + cross

    S, o = lax.scan(step, S0, (to_chunks(q, c), to_chunks(k, c), to_chunks(v, c)))
    return from_chunks(o), S

def peer_ffn(x, w_query, sub_keys, u_tab, v_tab):
    T, D = x.shape
    q = (x @ w_query).reshape(T, PEER_HEADS, 2, PEER_HALF)
    s = jnp.einsum('thpd,hpkd->thpk', q, sub_keys).astype(jnp.float32)
    s1, i1 = lax.top_k(s[:, :, 0], PEER_TOPK)
    s2, i2 = lax.top_k(s[:, :, 1], PEER_TOPK)
    n_cand = PEER_TOPK * PEER_TOPK
    cand_s = (s1[..., :, None] + s2[..., None, :]).reshape(T, PEER_HEADS, n_cand)
    cand_i = (i1[..., :, None] * PEER_NKEYS + i2[..., None, :]).reshape(T, PEER_HEADS, n_cand)
    top_s, top_pos = lax.top_k(cand_s, PEER_TOPK)
    e_idx = jnp.take_along_axis(cand_i, top_pos, axis=-1)
    gate = jax.nn.softmax(top_s, axis=-1)
    blk = math.gcd(T, PEER_BLOCK)
    nb = T // blk

    def block(args):
        xb, eb, gb = args
        a = jax.nn.gelu(jnp.einsum('thkd,td->thk', u_tab[eb], xb).astype(jnp.float32), approximate=False)
        return jnp.einsum('thk,thkd->td', (gb * a).astype(v_tab.dtype), v_tab[eb])

    out = lax.map(block, (x.reshape(nb, blk, D),
                          e_idx.reshape(nb, blk, PEER_HEADS, PEER_TOPK),
                          gate.reshape(nb, blk, PEER_HEADS, PEER_TOPK)))
    return out.reshape(T, D).astype(x.dtype)

def decoder_layer(x, pos0, C0, n0, m0, S0, rms_mix_g, w_in, b_ig, b_fg, norm_m_g, norm_r_g,
                  w_out, rms_ffn_g, w_query, sub_keys, peer_u, peer_v):
    B, L, D = x.shape
    f32 = jnp.float32
    xn = rmsnorm(x, rms_mix_g)
    p = (xn @ w_in).astype(f32)

    def heads(lo, nh, d):
        return p[..., lo:lo + nh * d].reshape(B, L, nh, d).transpose(0, 2, 1, 3)

    mq = heads(OFF_MQ, H_MLSTM, DK_MLSTM)
    mk = heads(OFF_MK, H_MLSTM, DK_MLSTM) * (DK_MLSTM ** -0.5)
    mv = heads(OFF_MV, H_MLSTM, DV_MLSTM)
    mo = jax.nn.sigmoid(p[..., OFF_MO:OFF_MO + W_MLSTM])
    ig = (p[..., OFF_MI:OFF_MI + H_MLSTM] + b_ig.astype(f32)).transpose(0, 2, 1)
    lf = jax.nn.log_sigmoid(p[..., OFF_MF:OFF_MF + H_MLSTM] + b_fg.astype(f32)).transpose(0, 2, 1)
    pos = pos0[:, None] + jnp.arange(L, dtype=jnp.int32)[None, :]
    rq = rotary(heads(OFF_RQ, H_RET, DK_RET), pos)
    rk = rotary(heads(OFF_RK, H_RET, DK_RET), pos) * (DK_RET ** -0.5)
    rv = heads(OFF_RV, H_RET, DV_RET)
    rg = p[..., OFF_RG:OFF_RG + W_RET]

    c = math.gcd(L, CHUNK)
    hm, C, n, m = mlstm_chunkwise(mq, mk, mv, ig, lf, C0.astype(f32), n0.astype(f32), m0.astype(f32), c)
    hr, S = retention_chunkwise(rq, rk, rv, S0.astype(f32), c)
    hm = hm.transpose(0, 2, 1, 3).reshape(B, L, W_MLSTM)
    hr = hr.transpose(0, 2, 1, 3).reshape(B, L, W_RET)
    mix = jnp.concatenate([mo * head_norm(hm, norm_m_g, H_MLSTM),
                           jax.nn.silu(rg) * head_norm(hr, norm_r_g, H_RET)], axis=-1)
    x = x + (mix.astype(x.dtype) @ w_out)
    hn = rmsnorm(x, rms_ffn_g)
    x = x + peer_ffn(hn.reshape(B * L, D), w_query, sub_keys, peer_u, peer_v).reshape(B, L, D)
    return x, C.astype(C0.dtype), n.astype(n0.dtype), m.astype(m0.dtype), S.astype(S0.dtype)

def setup_inputs(seed: int = 0) -> dict:
    key = jax.random.key(seed)
    ks = jax.random.split(key, 20)
    nrm = jax.random.normal
    f32 = jnp.float32
    return {
        'x_prompt': nrm(ks[0], (BATCH, SEQ, D_MODEL), f32),
        'x_sample': nrm(ks[1], (DEC_BATCH, DEC_SEQ, D_MODEL), f32),
        'state_mlstm_C': 0.1 * nrm(ks[2], (DEPTH, DEC_BATCH, H_MLSTM, DK_MLSTM, DV_MLSTM), f32),
        'state_mlstm_n': 0.1 * nrm(ks[3], (DEPTH, DEC_BATCH, H_MLSTM, DK_MLSTM), f32),
        'state_mlstm_m': nrm(ks[4], (DEPTH, DEC_BATCH, H_MLSTM), f32),
        'state_ret_S': nrm(ks[5], (DEPTH, DEC_BATCH, H_RET, DK_RET, DV_RET), f32),
        'pos_sample': jnp.full((DEC_BATCH,), PAST_LEN, dtype=jnp.int32),
        'rms_mix_g': 1.0 + 0.02 * nrm(ks[6], (DEPTH, D_MODEL), f32),
        'w_in': nrm(ks[7], (DEPTH, D_MODEL, PROJ_WIDTH), f32) * D_MODEL ** -0.5,
        'b_igate': 0.1 * nrm(ks[8], (DEPTH, H_MLSTM), f32),
        'b_fgate': jnp.linspace(3.0, 6.0, H_MLSTM, dtype=f32)[None, :] + 0.01 * nrm(ks[9], (DEPTH, H_MLSTM), f32),
        'norm_mlstm_g': 1.0 + 0.02 * nrm(ks[10], (DEPTH, W_MLSTM), f32),
        'norm_ret_g': 1.0 + 0.02 * nrm(ks[11], (DEPTH, W_RET), f32),
        'w_out': nrm(ks[12], (DEPTH, MIX_WIDTH, D_MODEL), f32) * MIX_WIDTH ** -0.5,
        'rms_ffn_g': 1.0 + 0.02 * nrm(ks[13], (DEPTH, D_MODEL), f32),
        'w_query': nrm(ks[14], (DEPTH, D_MODEL, PEER_HEADS * PEER_QDIM), f32) * D_MODEL ** -0.5,
        'sub_keys': nrm(ks[15], (DEPTH, PEER_HEADS, 2, PEER_NKEYS, PEER_HALF), f32) * PEER_HALF ** -0.5,
        'peer_u': nrm(ks[16], (DEPTH, PEER_EXPERTS, D_MODEL), f32) * D_MODEL ** -0.5,
        'peer_v': nrm(ks[17], (DEPTH, PEER_EXPERTS, D_MODEL), f32) * PEER_HEADS ** -0.5,
        'rms_final_g': 1.0 + 0.02 * nrm(ks[18], (D_MODEL,), f32),
    }

def reference(x_prompt, x_sample, state_mlstm_C, state_mlstm_n, state_mlstm_m, state_ret_S, pos_sample,
              rms_mix_g, w_in, b_igate, b_fgate, norm_mlstm_g, norm_ret_g, w_out, rms_ffn_g,
              w_query, sub_keys, peer_u, peer_v, rms_final_g):
    hp, hs = x_prompt, x_sample
    Bp = x_prompt.shape[0]
    sd = state_mlstm_C.dtype
    pos_prompt = jnp.zeros((Bp,), jnp.int32)
    pC, pn, pm, pS, sC, sn, sm, sS = [], [], [], [], [], [], [], []
    for l in range(DEPTH):
        w = (rms_mix_g[l], w_in[l], b_igate[l], b_fgate[l], norm_mlstm_g[l], norm_ret_g[l], w_out[l],
             rms_ffn_g[l], w_query[l], sub_keys[l], peer_u[l], peer_v[l])
        zC = jnp.zeros((Bp, H_MLSTM, DK_MLSTM, DV_MLSTM), sd)
        zn = jnp.zeros((Bp, H_MLSTM, DK_MLSTM), sd)
        zm = jnp.zeros((Bp, H_MLSTM), sd)
        zS = jnp.zeros((Bp, H_RET, DK_RET, DV_RET), state_ret_S.dtype)
        hp, C, n, m, S = decoder_layer(hp, pos_prompt, zC, zn, zm, zS, *w)
        pC.append(C); pn.append(n); pm.append(m); pS.append(S)
        hs, C, n, m, S = decoder_layer(hs, pos_sample, state_mlstm_C[l], state_mlstm_n[l], state_mlstm_m[l],
                                       state_ret_S[l], *w)
        sC.append(C); sn.append(n); sm.append(m); sS.append(S)
    y_prompt = rmsnorm(hp, rms_final_g)
    y_sample = rmsnorm(hs, rms_final_g)
    return (y_prompt, y_sample, jnp.stack(pC), jnp.stack(pn), jnp.stack(pm), jnp.stack(pS),
            jnp.stack(sC), jnp.stack(sn), jnp.stack(sm), jnp.stack(sS))


_drawn_inputs = setup_inputs


def setup_inputs(seed=0):
    import zlib

    import numpy as np

    out = dict(_drawn_inputs(seed))
    spreads = {}
    factors = {'norm_mlstm_g': 37.76, 'norm_ret_g': 35.83, 'rms_final_g': 23.774, 'rms_ffn_g': 16.07}
    for name, (base, spread) in spreads.items():
        noise = np.random.default_rng([zlib.crc32(name.encode()), seed]).standard_normal(out[name].shape)
        drawn = base * np.exp(spread * noise) if base else spread * noise
        out[name] = __import__('jax').numpy.asarray(drawn.astype(out[name].dtype))
    for name, factor in factors.items():
        out[name] = (out[name] * factor).astype(out[name].dtype)
    return out
```

```python
from contextlib import ExitStack

import numpy as np
import concourse.bass as bass
from concourse import mybir

F32 = mybir.dt.float32
F32R = mybir.dt.float32r
U32 = mybir.dt.uint32
I32 = mybir.dt.int32
ALU = mybir.AluOpType
ACT = mybir.ActivationFunctionType
AX = mybir.AxisListType

P = 128
D = 1024
ND = D // P
SEQ = 1024
NC = SEQ // P
NS = 8
T = SEQ + NS
NT = NC + 1
H = 4
EPS = 1e-6
SCALE = float(P) ** -0.5
PH, NK, TOPK = 8, 128, 16
GROUPS = [range(0, 4), range(4, NC), range(NC, NT)]
SUB = 64
NSUB = SEQ // SUB
LOW = -3.0e38
PROJ = 520
Q0, K0, V0, ONE0, O0 = 0, P, 2 * P, 3 * P, 3 * P + 1
NEG = -1.0e30


def rows(t):
    return P if t < NC else NS


class Chain:

    def __init__(self, eng, sem, start=0):
        self.eng, self.sem, self.n, self.start = eng, sem, 0, start
        self.loop, self.per = None, 0

    def enter(self, i, per):
        self.start += self.n
        self.loop, self.per, self.n = i, per, 0

    def leave(self, passes):
        assert self.n == self.per, (self.n, self.per)
        self.start += self.per * passes
        self.loop, self.n = None, 0

    def value(self, n=None):
        n = self.n if n is None else n
        return self.start + n if self.loop is None else self.loop * self.per + (self.start + n)

    def link(self, ins):
        ins.then_inc(self.sem, 1)
        self.n += 1
        self.wait(self.n)
        return self.n

    def mark(self, ins):
        ins.then_inc(self.sem, 1)
        self.n += 1
        return self.n

    def wait(self, n):
        self.eng.wait_ge(self.sem, self.value(n))


UNITS = [(dk, g) for g in range(2) for dk in range(ND)] + [(0, 2)]


def transpose_units_pe(nc, pe, src, ident, bank, tr_done, tr_free, ready):
    for u, (dk, g) in enumerate(UNITS):
        if dk == 0:
            ready(g)
        if u >= len(bank):
            pe.wait_ge(tr_free, u - len(bank) + 1)
        b = bank[u % len(bank)]
        if g < 2:
            for k in range(4):
                t = 4 * g + k
                last = nc.tensor.transpose(b[:, k * P:(k + 1) * P], src[:, t, dk * P:(dk + 1) * P], ident[:, :])
        else:
            for k in range(ND):
                last = nc.tensor.transpose(b[:, k * NS:(k + 1) * NS], src[:NS, NC, k * P:(k + 1) * P],
                                           ident[:NS, :NS])
        last.then_inc(tr_done, 1)


def transpose_units_out(nc, dve, dst, gcol, bank, tr_done, tr_free):
    for u, (dk, g) in enumerate(UNITS):
        dve.wait_ge(tr_done, u + 1)
        b = bank[u % len(bank)]
        if g < 2:
            nc.vector.tensor_scalar(dst[:, dk, 4 * g * P:(4 * g + 4) * P], b[:, :], gcol[:, dk:dk + 1], None,
                                    ALU.mult).then_inc(tr_free, 1)
        else:
            nc.vector.tensor_tensor(dst[:, :, SEQ:T], b[:, 0:ND * NS].rearrange("p (k n) -> p k n", k=ND),
                                    gcol[:, :].unsqueeze(2).broadcast_to([P, ND, NS]),
                                    ALU.mult).then_inc(tr_free, 1)


def build(nc, A, O):
    with ExitStack() as top:
        def sb(ctx, name, shape, dt=F32):
            return ctx.enter_context(nc.sbuf_tensor(name, shape, dt))

        def ps(ctx, name, shape=(P, 512), dt=F32):
            return ctx.enter_context(nc.psum_tensor(name, list(shape), dt))

        held = {}

        def sem(name):
            if name not in held:
                held[name] = top.enter_context(nc.semaphore(name))
            return held[name]

        def clear(prefix):
            with nc.Block() as block:
                @block.vector
                def _(dve):
                    for name in held:
                        if name.startswith(prefix):
                            dve.sem_clear(held[name])

        x2_dram = nc.dram_tensor("x2_scratch", (T, D), F32, kind="Internal").ap()
        g_dram = nc.dram_tensor("gate_scratch", (NSUB, NK, NK, SUB), F32, kind="Internal").ap()

        ident = sb(top, "ident", [P, P])
        x2_saved = sem("x2_saved")
        hnT = sb(top, "hnT", [P, ND, T])
        g_tail = sb(top, "g_tail", [NK, NK, NS])
        with ExitStack() as mixer:
            mixer_stages(nc, A, O, mixer, sb, ps, sem, clear, ident, hnT, x2_dram, x2_saved)
        with ExitStack() as routing:
            routing_stages(nc, A, routing, sb, ps, sem, ident, hnT, g_dram, g_tail)
        for group in range(2):
            if group:
                clear("x_")
            with ExitStack() as sweep:
                expert_sweep(nc, A, O, sweep, sb, ps, sem, ident, hnT, g_dram, g_tail, x2_dram, group)


def mixer_stages(nc, A, O, own, sb, ps, sem, clear, ident, hnT, x2_dram, x2_saved):
    mix = sb(own, "mix", [P, NT, D])
    xnT = hnT
    gain = sb(own, "gain", [P, 4, ND])
    cols = sb(own, "cols", [P, NT, 4, H])
    dec = sb(own, "dec", [P, H, 2 * NC])
    negmd = sb(own, "negmd", [H, H, SEQ])
    gmix, gnm, gffn = gain[:, 0, :], gain[:, 1, :], gain[:, 2, :]

    with ExitStack() as st, nc.Block() as block:
        junk = sb(st, "sq_junk", [P, D])
        ss = sb(st, "ss", [P, NT])
        rstd = sb(st, "rstd", [P, NT])
        xn = sb(st, "xn", [P, NT, D])
        bank = [ps(st, f"n_tr{i}") for i in range(4)]
        x_in = [sem(f"x_in{t}") for t in range(NT)]
        const_in, ones_set, sq_done, ms_done, root_done, rstd_done, xn_done, tr_done, tr_free = (
            sem(n) for n in ("const_in", "ones_set", "sq_done", "ms_done", "root_done", "rstd_done", "xn_done",
                             "n_tr_done", "n_tr_free"))

        @block.sync
        def _(sp):
            for t in range(NT):
                sp.dma_start(mix[:rows(t), t, :], A["x"][t * P:t * P + rows(t), :]).then_inc(x_in[t], 16)
            sp.dma_start(ident[:, :], A["ident"]).then_inc(const_in, 16)
            sp.dma_start(gain[:, :, :], A["gains"]).then_inc(const_in, 16)

        @block.scalar
        def _(act):
            act.wait_ge(ones_set, 1)
            for t in range(NT):
                act.wait_ge(x_in[t], 16)
                if t:
                    act.wait_ge(sq_done, t)
                nc.scalar.activation(junk[:rows(t), :], mix[:rows(t), t, :], ACT.Square,
                                     accum_out=ss[:rows(t), t:t + 1]).then_inc(sq_done, 1)
            act.wait_ge(ms_done, 1)
            nc.scalar.activation(rstd[:, :], ss[:, :], ACT.Sqrt).then_inc(root_done, 1)
            act.wait_ge(rstd_done, 1)
            for t in range(NT):
                nc.scalar.activation(xn[:rows(t), t, :], mix[:rows(t), t, :], ACT.Copy,
                                     scale=rstd[:rows(t), t:t + 1]).then_inc(xn_done, 1)

        @block.vector
        def _(dve):
            nc.vector.memset(ss[:, :], 1.0).then_inc(ones_set, 1)
            dve.wait_ge(sq_done, NT)
            nc.vector.tensor_scalar(ss[:, :], ss[:, :], 1.0 / D, EPS, ALU.mult, ALU.add).then_inc(ms_done, 1)
            dve.wait_ge(root_done, 1)
            nc.vector.reciprocal(rstd[:, :], rstd[:, :]).then_inc(rstd_done, 1)
            dve.wait_ge(const_in, 32)
            transpose_units_out(nc, dve, xnT, gmix, bank, tr_done, tr_free)

        @block.tensor
        def _(pe):
            pe.wait_ge(const_in, 32)
            transpose_units_pe(nc, pe, xn, ident, bank, tr_done, tr_free,
                               lambda g: pe.wait_ge(xn_done, (4, 8, NT)[g]))

    with ExitStack() as st, nc.Block() as block:
        wif = sb(st, "wif", [P, ND, 2 * H])
        bif = sb(st, "bif", [H, 2])
        msk = sb(st, "chunk_start_mask", [H, T])
        delta = sb(st, "delta4", [H, H])
        ones4 = sb(st, "ones4a", [H, P])
        m_in = sb(st, "m_in", [H, NS])
        ig = sb(st, "ig", [H, T])
        zf = sb(st, "zf", [H, T])
        ez = sb(st, "ez", [H, T])
        lf = sb(st, "lf", [H, T])
        b = sb(st, "b", [H, T])
        shift = sb(st, "shift", [H, SEQ])
        M = sb(st, "M", [H, T])
        row = sb(st, "row", [H, 4, T])
        mnew = sb(st, "mnew", [H, NC + NS])
        mprev = sb(st, "mprev", [H, NC])
        decmd = sb(st, "decmd", [H, H, 2 * NC])
        pi = [ps(st, f"g_i{i}") for i in range(3)]
        pf = [ps(st, f"g_f{i}") for i in range(3)]
        pc, pd = ps(st, "g_cols"), ps(st, "g_dec")
        gate_in, pre_done, z_done, e1_done, e2_done, rows_done, cols_ps, cols_out, dec_ps, exp_out, m_out, chain = (
            sem(n) for n in ("gate_in", "gate_pre", "gate_z", "gate_exp", "gate_ln", "gate_rows", "cols_ps",
                             "cols_out", "dec_ps", "cols_exp", "m_out", "gate_chain"))
        TC = T // 3

        @block.sync
        def _(sp):
            for dst, src in ((wif[:, :, :], A["w_if"]), (bif[:, :], A["b_if"]), (msk[:, :], A["start_mask"]),
                             (delta[:, :], A["delta4"]), (m_in[:, :], A["m_in"]), (ones4[:, :], A["ones4"])):
                sp.dma_start(dst, src).then_inc(gate_in, 16)
            sp.wait_ge(rows_done, 1)
            sp.dma_start(O["m"], mnew[:, NC - 1:NC + NS]).then_inc(m_out, 16)
            sp.wait_ge(m_out, 16)

        @block.tensor
        def _(pe):
            pe.wait_ge(gate_in, 96)
            for c in range(3):
                for g, bk in ((0, pi), (1, pf)):
                    for k in range(ND):
                        last = nc.tensor.matmul(bk[c][:H, 0:TC], wif[:, k, g * H:(g + 1) * H],
                                                xnT[:, k, c * TC:(c + 1) * TC], start=(k == 0), stop=(k == ND - 1))
            last.then_inc(pre_done, 1)
            pe.wait_ge(rows_done, 1)
            for t in range(NT):
                for q in range(4):
                    last = nc.tensor.transpose(pc[:rows(t), (t * 4 + q) * H:(t * 4 + q + 1) * H],
                                               row[:, q, t * P:t * P + rows(t)], ident[:H, :H])
            last.then_inc(cols_ps, 1)
            nc.tensor.matmul(pd[:, 0:H * 2 * NC], ones4[:, :], decmd[:, :, :].rearrange("p h c -> p (h c)"),
                             start=True, stop=True).then_inc(dec_ps, 1)

        @block.scalar
        def _(act):
            act.wait_ge(z_done, 1)
            nc.scalar.activation(ez[:, :], ez[:, :], ACT.Exp, scale=-1.0).then_inc(e1_done, 1)
            act.wait_ge(e1_done, 1)
            nc.scalar.activation(ez[:, :], ez[:, :], ACT.Ln, bias=1.0).then_inc(e2_done, 1)
            act.wait_ge(cols_out, 1)
            nc.scalar.activation(cols[:, :, 1:4, :], cols[:, :, 1:4, :], ACT.Exp).then_inc(exp_out, 1)
            act.wait_ge(dec_ps, 1)
            nc.scalar.activation(dec[:, :, :], pd[:, 0:H * 2 * NC].rearrange("p (h c) -> p h c", h=H),
                                 ACT.Exp).then_inc(exp_out, 1)

        @block.vector
        def _(dve):
            v = nc.vector
            ch = Chain(dve, chain)
            dve.wait_ge(gate_in, 96)
            ch.mark(v.memset(shift[:, :], 0.0))
            ch.mark(v.memset(mprev[:, :], 0.0))
            ch.mark(v.memset(cols[:, :, :, :], 0.0))
            dve.wait_ge(pre_done, 1)
            for c in range(3):
                s = slice(c * TC, (c + 1) * TC)
                ch.mark(v.tensor_scalar(ig[:, s], pi[c][:H, 0:TC], bif[:, 0:1], None, ALU.add))
                ch.link(v.tensor_scalar(zf[:, s], pf[c][:H, 0:TC], bif[:, 1:2], None, ALU.add))
            v.scalar_tensor_tensor(ez[:, :], zf[:, :], -1.0, zf[:, :], ALU.mult, ALU.max).then_inc(z_done, 1)
            dve.wait_ge(e2_done, 1)
            ch.link(v.scalar_tensor_tensor(lf[:, :], zf[:, :], 0.0, ez[:, :], ALU.min, ALU.subtract))
            ch.link(v.tensor_tensor_scan(b[:, :], msk[:, :], lf[:, :], 0.0, ALU.mult, ALU.add))
            ch.mark(v.tensor_tensor(row[:, 0, :], ig[:, :], b[:, :], ALU.subtract))
            bl = b[:, 0:SEQ].rearrange("p (c t) -> p c t", t=P)[:, :, P - 1]
            ch.link(v.tensor_copy(shift[:, P:SEQ].rearrange("p (c t) -> p c t", t=P)[:, :, 0], bl[:, 0:NC - 1]))
            ch.mark(v.tensor_tensor_scan(M[:, 0:SEQ], shift[:, :], row[:, 0, 0:SEQ], 0.0, ALU.add, ALU.max))
            ch.link(v.tensor_tensor(M[:, SEQ:T], m_in[:, :], row[:, 0, SEQ:T], ALU.max))
            M3 = M[:, 0:SEQ].rearrange("p (c t) -> p c t", t=P)
            ml = M3[:, :, P - 1]
            ch.mark(v.tensor_tensor(mnew[:, NC:NC + NS], M[:, SEQ:T], b[:, SEQ:T], ALU.add))
            ch.link(v.tensor_tensor(mnew[:, 0:NC], ml, bl, ALU.add))
            ch.link(v.tensor_copy(mprev[:, 1:NC], mnew[:, 0:NC - 1]))

            def c3(ap):
                return ap[:, 0:SEQ].rearrange("p (c t) -> p c t", t=P)
            ch.mark(v.tensor_tensor(c3(row[:, 1, :]), mprev[:, :].unsqueeze(2).broadcast_to([H, NC, P]), M3,
                                    ALU.subtract))
            ch.mark(v.tensor_tensor(row[:, 1, SEQ:T], m_in[:, :], M[:, SEQ:T], ALU.subtract))
            ch.mark(v.scalar_tensor_tensor(row[:, 2, :], M[:, :], -1.0, b[:, :], ALU.mult, ALU.subtract))
            ch.mark(v.tensor_tensor(c3(row[:, 3, :]), c3(row[:, 0, :]), ml.unsqueeze(2).broadcast_to([H, NC, P]),
                                    ALU.subtract))
            ch.link(v.tensor_tensor(row[:, 3, SEQ:T], row[:, 0, SEQ:T], M[:, SEQ:T], ALU.subtract))
            for h in range(H):
                ch.mark(v.tensor_scalar(negmd[:, h, :], M[:, 0:SEQ], delta[:, h:h + 1], -1.0, ALU.mult, ALU.mult))
                ch.mark(v.tensor_scalar(decmd[:, h, 0:NC], c3(row[:, 1, :])[:, :, P - 1], delta[:, h:h + 1], None,
                                        ALU.mult))
                last = v.tensor_scalar(decmd[:, h, NC:2 * NC], row[:, 1, SEQ:T], delta[:, h:h + 1], None, ALU.mult)
            last.then_inc(rows_done, 1)
            dve.wait_ge(cols_ps, 1)
            pc4 = pc[:, 0:NT * 16].rearrange("p (t q h) -> p t q h", q=4, h=H)
            ch.link(v.tensor_copy(cols[:, 0:NC, :, :], pc4[:, 0:NC]))
            v.tensor_copy(cols[:NS, NC, :, :], pc4[:NS, NC]).then_inc(cols_out, 1)

    consts = own.enter_context(ExitStack())
    head_loop(nc, A, O, sb, ps, sem, ident, xnT, mix, cols, dec, negmd, False)
    clear("h_")
    head_loop(nc, A, O, sb, ps, sem, ident, xnT, mix, cols, dec, negmd, True)

    with ExitStack() as st, nc.Block() as block:
        mixT = sb(st, "mixT", [P, ND, T])
        wo = sb(st, "wo", [P, ND, D])
        x2 = sb(st, "x2", [P, NT, D])
        junk = sb(st, "sq_junk2", [P, D])
        ss = sb(st, "ss2", [P, NT])
        rstd = sb(st, "rstd2", [P, NT])
        bank = [ps(st, f"o_tr{i}") for i in range(4)]
        py = [ps(st, f"o_y{i}") for i in range(4)]
        x_in = sem("x2_in")
        wo_in, ones_set, mt_done, mt_free, y_done, x2_done, sq_done, ms_done, root_done, rstd_done, hn_done, h_done, h_free = (
            sem(n) for n in ("wo_in", "o_ones", "o_mt_done", "o_mt_free", "o_y_done", "o_x2", "o_sq", "o_ms",
                             "o_root", "o_rstd", "o_hn", "o_h_done", "o_h_free"))

        @block.sync
        def _(sp):
            sp.dma_start(wo[:, :, :], A["w_out"]).then_inc(wo_in, 16)
            for t in range(NT):
                sp.dma_start(x2[:rows(t), t, :], A["x"][t * P:t * P + rows(t), :]).then_inc(x_in, 16)
            for t in range(NT):
                sp.wait_ge(x2_done, 2 * t + 2)
                sp.dma_start(x2_dram[t * P:t * P + rows(t), :], x2[:rows(t), t, :]).then_inc(x2_saved, 16)
            sp.wait_ge(x2_saved, 16 * NT)

        @block.tensor
        def _(pe):
            transpose_units_pe(nc, pe, mix, ident, bank, mt_done, mt_free, lambda g: None)
            pe.wait_ge(wo_in, 16)
            pe.wait_ge(mt_free, len(UNITS))
            for t in range(NT):
                for n in range(2):
                    u = 2 * t + n
                    if u >= 4:
                        pe.wait_ge(x2_done, u - 3)
                    for k in range(ND):
                        last = nc.tensor.matmul(py[u % 4][:rows(t), :], mixT[:, k, t * P:t * P + rows(t)],
                                                wo[:, k, n * 512:(n + 1) * 512], start=(k == 0), stop=(k == ND - 1))
                    last.then_inc(y_done, 1)
            transpose_units_pe(nc, pe, mix, ident, bank, h_done, h_free, lambda g: pe.wait_ge(hn_done, (4, 8, NT)[g]))

        @block.scalar
        def _(act):
            act.wait_ge(ones_set, 1)
            for t in range(NT):
                act.wait_ge(x2_done, 2 * t + 2)
                if t:
                    act.wait_ge(sq_done, t)
                nc.scalar.activation(junk[:rows(t), :], x2[:rows(t), t, :], ACT.Square,
                                     accum_out=ss[:rows(t), t:t + 1]).then_inc(sq_done, 1)
            act.wait_ge(ms_done, 1)
            nc.scalar.activation(rstd[:, :], ss[:, :], ACT.Sqrt).then_inc(root_done, 1)
            act.wait_ge(rstd_done, 1)
            for t in range(NT):
                nc.scalar.activation(mix[:rows(t), t, :], x2[:rows(t), t, :], ACT.Copy,
                                     scale=rstd[:rows(t), t:t + 1]).then_inc(hn_done, 1)

        @block.vector
        def _(dve):
            nc.vector.memset(ss[:, :], 1.0).then_inc(ones_set, 1)
            transpose_units_out(nc, dve, mixT, gnm, bank, mt_done, mt_free)
            dve.wait_ge(x_in, 16 * NT)
            for t in range(NT):
                for n in range(2):
                    u = 2 * t + n
                    s = slice(n * 512, (n + 1) * 512)
                    dve.wait_ge(y_done, u + 1)
                    nc.vector.tensor_tensor(x2[:rows(t), t, s], py[u % 4][:rows(t), :], x2[:rows(t), t, s],
                                            ALU.add).then_inc(x2_done, 1)
            dve.wait_ge(sq_done, NT)
            nc.vector.tensor_scalar(ss[:, :], ss[:, :], 1.0 / D, EPS, ALU.mult, ALU.add).then_inc(ms_done, 1)
            dve.wait_ge(root_done, 1)
            nc.vector.reciprocal(rstd[:, :], rstd[:, :]).then_inc(rstd_done, 1)
            transpose_units_out(nc, dve, hnT, gffn, bank, h_done, h_free)


def head_loop(nc, A, O, sb, ps, sem, ident, xnT, mix, cols, dec, negmd, ret):
    n0 = "r" if ret else "m"
    base = H if ret else 0
    W = P if ret else P + 1
    with ExitStack() as st, nc.Block() as block:
        w = sb(st, n0 + "_w", [P, 2, ND, 512])
        pr = sb(st, n0 + "_pr", [P, NT, PROJ])
        gate = sb(st, n0 + "_gate", [P, 2, NT, P])
        dm = sb(st, n0 + "_dm", [P, H if ret else 1, SEQ if not ret else P])
        hh = sb(st, n0 + "_h", [P, NT, P])
        hx = sb(st, n0 + "_hx", [P, P + 1])
        den = sb(st, n0 + "_den", [P, 2])
        stats = sb(st, n0 + "_stats", [P, NT, 6])
        mv = sb(st, n0 + "_mv", [P, NT, 2])
        qkT = sb(st, n0 + "_qkT", [P, 2, 2 * P])
        sd = sb(st, n0 + "_sd", [P, P])
        ka = sb(st, n0 + "_ka", [P, P])
        C = sb(st, n0 + "_C", [P, H, W])
        cs = sb(st, n0 + "_cs", [P, H, NS, W])
        kbig = sb(st, n0 + "_kbig", [NS, NS, P])
        qm = sb(st, n0 + "_qm", [P, NS, P])
        dmask = sb(st, n0 + "_dmask", [NS, NS, P])
        if ret:
            rot = sb(st, "r_rot", [P, NT, 2, 2, P // 2])
            cosin = sb(st, "r_cosin", [P, 2, NT, P // 2])
            m1 = sb(st, "r_m1", [P, 2, 2, P // 2])
            m2 = sb(st, "r_m2", [P, 2, 2, P // 2])
            rcol = sb(st, "r_col", [P, 3, H])
            rdec1 = sb(st, "r_dec1", [P, H])
            pos = sb(st, "r_pos", [NS, 1], I32)
            posf = sb(st, "r_posf", [NS, 1])
            inv = sb(st, "r_inv", [NS, P // 2])
            ang = sb(st, "r_ang", [NS, 2, P // 2])
            turns = sb(st, "r_turns", [NS, 2, P // 2])
        else:
            neg = sb(st, "m_neg", [P, P])
            ones4 = sb(st, "m_ones4", [H, P])
            pb = ps(st, "m_pb", (P, 1024))
        pp = [ps(st, f"{n0}_pp{i}") for i in range(2)]
        pt, pS, pA, pU = (ps(st, f"{n0}_p{i}") for i in "tSAU")
        names = ("w_in0 w_in1 const_in preset bc_done arg_done dm_done pj_done pj_out tr_done "
                 "tr_out rot_done s_done sd_done ka_done a_done h_done u_done c_done kb_done "
                 "up_done cs_done hs_done heads_done root_done out_c out_cs chain cs_in var_done").split()
        S = {n: sem("h_" + n) for n in names}
        TOK = [0, 1, 2, 3, NC, 4, 5, 6, 7]

        @block.sync
        def _(sp):
            loads = [(dmask[:, :, :], A["dmask"])]
            if ret:
                loads += [(dm[:, :, :], A["dmat"]), (cosin[:, :, 0:NC, :], A["cosin"]), (rcol[:, :, :], A["rcol"]),
                          (rdec1[:, :], A["rdec1"]), (pos[:, :], A["pos"]), (inv[:, :], A["inv"])]
            else:
                loads += [(neg[:, :], A["neg"]), (ones4[:, :], A["ones4"])]
            for dst, src in loads:
                sp.dma_start(dst, src).then_inc(S["const_in"], 16)
            sp.sem_inc(S["w_in1"], 16)
            for s in range(2):
                sp.dma_start(w[:, s, :, :], A["w_heads"][base + s]).then_inc(S[f"w_in{s}"], 16)
            sp.dma_start(cs[:, :, :, :], A["cs" + n0]).then_inc(S["cs_in"], 16)
            for h in range(H):
                if h < 2:
                    sp.wait_ge(S["pj_done"], NT * (h + 1))
                    sp.dma_start(w[:, h % 2, :, :], A["w_heads"][base + h + 2]).then_inc(S[f"w_in{h % 2}"], 16)
                sp.wait_ge(S["cs_done"], NS * (h + 1))
                sp.dma_start(O["cs" + n0][h], cs[:, h, :, :]).then_inc(S["out_cs"], 16)
                sp.wait_ge(S["c_done"], NC * (h + 1) + 1)
                sp.dma_start(O["c" + n0][h], C[:, h, :]).then_inc(S["out_c"], 16)
            sp.wait_ge(S["out_c"], 16 * H)
            sp.wait_ge(S["out_cs"], 16 * H)

        @block.tensor
        def _(pe):
            mm, tp = nc.tensor.matmul, nc.tensor.transpose
            pe.sem_inc(S["hs_done"], 1)
            pe.sem_inc(S["a_done"], 1)
            pe.wait_ge(S["const_in"], 16 * (7 if ret else 3))
            with pe.Fori(0, H) as h:
                hb = h % 2

                def project(i, part):
                    if i >= NT:
                        return
                    t = TOK[i]
                    if part == 0:
                        if i == 0:
                            pe.wait_ge(S["w_in0"], ((h + 2) // 2) * 16)
                            pe.wait_ge(S["w_in1"], ((h + 3) // 2) * 16)
                    for k in range(4 * part, 4 * part + 4):
                        last = mm(pp[i % 2][:rows(t), :], xnT[:, k, t * P:t * P + rows(t)], w[:, hb, k, :],
                                  start=(k == 0), stop=(k == ND - 1))
                    if part == 1:
                        last.then_inc(S["pj_done"], 1)

                if not ret:
                    for i in range(2):
                        last = mm(pb[:, i * 512:(i + 1) * 512], ones4[:, :], negmd[:, h, i * 512:(i + 1) * 512],
                                  start=True, stop=True)
                    last.then_inc(S["bc_done"], 1)
                for i in range(2):
                    for part in range(2):
                        project(i, part)
                for i, t in enumerate(TOK):
                    if ret:
                        pe.wait_ge(S["rot_done"], 2 * (h * NT + i + 1))
                    else:
                        pe.wait_ge(S["pj_out"], h * NT + i + 1)
                    for q in range(2 if t < NC else 1):
                        src = rot[:, t, q, :, :].rearrange("p a b -> p (a b)") if ret else pr[:, t, q * P:(q + 1) * P]
                        last = tp(pt[:, q * P:(q + 1) * P], src, ident[:, :])
                    last.then_inc(S["tr_done"], 1)
                    project(i + 2, 0)
                    pe.wait_ge(S["tr_out"], h * NT + i + 1)
                    if t < NC:
                        mm(pS[:, 0:P], qkT[:, t % 2, P:2 * P], qkT[:, t % 2, 0:P], start=True,
                           stop=True).then_inc(S["s_done"], 1)
                        pe.wait_ge(S["ka_done"], h * NC + t + 1)
                        pe.wait_ge(S["c_done"], h * NC + t + 1)
                        mm(pU[:, 0:W], ka[:, :], pr[:, t, V0:V0 + W], start=True, stop=True).then_inc(S["u_done"], 1)
                        project(i + 2, 1)
                        pe.wait_ge(S["sd_done"], h * NC + t + 1)
                        pe.wait_ge(S["h_done"], h * NT + i + 1)
                        last = mm(pA[:, 0:W], sd[:, :], pr[:, t, V0:V0 + W], start=True, stop=True)
                        if t:
                            last = mm(pA[:, 256:256 + W], qkT[:, t % 2, 0:P], C[:, h, :], start=True, stop=True)
                        last.then_inc(S["a_done"], 1)
                    else:
                        pe.wait_ge(S["kb_done"], h + 1)
                        pe.wait_ge(S["c_done"], h * NC + TOK.index(NC) + 1)
                        pe.wait_ge(S["sd_done"], h * NC + TOK.index(NC))
                        for n in range(NS):
                            if n >= 2:
                                pe.wait_ge(S["cs_done"], h * NS + n - 1)
                            mm((pU, pS)[n % 2][:, 0:W], kbig[:, n, :], pr[:NS, NC, V0:V0 + W], start=True,
                               stop=True).then_inc(S["up_done"], 1)
                        project(i + 2, 1)
                        pe.wait_ge(S["cs_done"], h * NS + NS)
                        pe.wait_ge(S["h_done"], h * NT + i + 1)
                        for n in range(NS):
                            last = mm(pA[:, 0:W], qm[:, n, :], cs[:, h, n, :], start=(n == 0), stop=(n == NS - 1))
                        last.then_inc(S["hs_done"], 1)

        @block.scalar
        def _(act):
            ac = nc.scalar.activation
            act.wait_ge(S["preset"], 1)
            if ret:
                act.wait_ge(S["preset"], 2)
                ac(cosin[:NS, 1, NC, :], ang[:, 1, :], ACT.Sin)
                ac(cosin[:NS, 0, NC, :], ang[:, 0, :], ACT.Sin).then_inc(S["preset"], 1)
            with act.Fori(0, H) as h:
                act.wait_ge(S["heads_done"], h + 1)
                act.wait_ge(S["hs_done"], h + 1)
                for i, t in enumerate(TOK):
                    r = rows(t)
                    act.wait_ge(S["pj_done"], h * NT + i + 1)
                    ac(gate[:r, h % 2, t, :], pp[i % 2][:r, 3 * P:4 * P], ACT.Silu if ret else ACT.Sigmoid)
                    ac(pr[:r, t, 0:3 * P], pp[i % 2][:r, 0:3 * P], ACT.Copy).then_inc(S["pj_out"], 1)
                    if t == 0 and not ret:
                        act.wait_ge(S["arg_done"], h * NC + NC)
                        ac(dm[:, 0, :], dm[:, 0, :], ACT.Exp).then_inc(S["dm_done"], 1)
                    act.wait_ge(S["tr_done"], h * NT + i + 1)
                    if t == 0:
                        act.wait_ge(S["a_done"], h * NC + 1)
                    elif t >= 2:
                        act.wait_ge(S["a_done"], h * NC + (t if t < NC else 1))
                    if t < NC:
                        ac(qkT[:, t % 2, :], pt[:, 0:2 * P], ACT.Copy).then_inc(S["tr_out"], 1)
                    else:
                        ac(qm[:, :, :].rearrange("p a b -> p (a b)")[:, 0:NS * P:P + 1], pt[:, 0:NS],
                           ACT.Copy).then_inc(S["tr_out"], 1)
                act.wait_ge(S["var_done"], h + 1)
                ac(mv[:, :, 1], mv[:, :, 1], ACT.Sqrt).then_inc(S["root_done"], 1)

        @block.vector
        def _(dve):
            v = nc.vector
            ch = Chain(dve, S["chain"])
            ch.mark(v.memset(qm[:, :, :], 0.0))
            ch.mark(v.memset(stats[:, :, :], 1.0))
            if ret:
                ch.mark(v.memset(rot[:, NC], 1.0))
            ch.mark(v.memset(hh[:, :, :], 0.0))
            ch.mark(v.memset(gate[:, :, :, :], 1.0))
            dve.sem_inc(S["c_done"], 1)
            dve.sem_inc(S["h_done"], 1)
            dve.sem_inc(S["heads_done"], 2)
            v.memset(pr[:, :, :], 1.0).then_inc(S["preset"], 1)
            dve.wait_ge(S["const_in"], 16 * (7 if ret else 3))
            if ret:
                TP = [6.28125, 253 / 131072, 2 * np.pi - 6.28125 - 253 / 131072]
                ch.link(v.tensor_copy(posf[:, :], pos[:, :]))
                ch.link(v.tensor_scalar(ang[:, 1, :], inv[:, :], posf[:, 0:1], None, ALU.mult))
                ch.link(v.tensor_scalar(turns[:, 1, :], ang[:, 1, :], float(1 / (2 * np.pi)), 0.0, ALU.mult, ALU.add))
                ch.link(v.tensor_scalar(turns[:, 0, :], turns[:, 1, :], 0.25, 12582912.0, ALU.add, ALU.add))
                ch.link(v.tensor_scalar(turns[:, 1, :], turns[:, 1, :], 12582912.0, -12582912.0, ALU.add, ALU.add))
                ch.link(v.tensor_scalar(turns[:, 0, :], turns[:, 0, :], -12582912.0, 0.0, ALU.add, ALU.add))
                ch.link(v.tensor_copy(ang[:, 0, :], ang[:, 1, :]))
                for c in TP:
                    ch.link(v.scalar_tensor_tensor(ang[:, :, :], turns[:, :, :], -float(np.float32(c)), ang[:, :, :],
                                                   ALU.mult, ALU.add))
                ch.link(v.tensor_scalar(ang[:, 0, :], ang[:, 0, :], float(np.pi / 2), 0.0, ALU.add, ALU.add))
                v.tensor_scalar(ang[:, :, :], ang[:, :, :], 3.1415925, -3.1415925, ALU.min,
                                ALU.max).then_inc(S["preset"], 1)
                dve.wait_ge(S["preset"], 3)
            with dve.Fori(0, H) as h:
                ch.enter(h, PER["ret" if ret else "mlstm"])
                g0 = h + base
                if not ret:
                    dve.wait_ge(S["bc_done"], h + 1)
                    for c in range(NC):
                        v.scalar_tensor_tensor(dm[:, 0, c * P:(c + 1) * P], pb[:, c * P:(c + 1) * P],
                                               cols[:, c, 0, bass.ds(h, 1)], neg[:, :], ALU.add,
                                               ALU.min).then_inc(S["arg_done"], 1)

                def rotate(i):
                    t = TOK[i]
                    r = rows(t)
                    dve.wait_ge(S["pj_out"], h * NT + i + 1)
                    cos = cosin[:r, 0, t, :].unsqueeze(1).broadcast_to([r, 4, P // 2])
                    sin = cosin[:r, 1, t, :].unsqueeze(1).broadcast_to([r, 4, P // 2])
                    qk4 = pr[:r, t, 0:2 * P].rearrange("p (i b) -> p i b", i=4)
                    ch.mark(v.tensor_tensor(m1[:r].rearrange("p i a b -> p (i a) b"), qk4, cos, ALU.mult))
                    ch.link(v.tensor_tensor(m2[:r].rearrange("p i a b -> p (i a) b"), qk4, sin, ALU.mult))
                    v.tensor_tensor(rot[:r, t, :, 0, :], m1[:r, :, 0, :], m2[:r, :, 1, :],
                                    ALU.subtract).then_inc(S["rot_done"], 1)
                    v.tensor_tensor(rot[:r, t, :, 1, :], m2[:r, :, 0, :], m1[:r, :, 1, :],
                                    ALU.add).then_inc(S["rot_done"], 1)

                if ret:
                    rotate(0)
                for i, t in enumerate(TOK):
                    r = rows(t)
                    if ret:
                        winter, acol, dcol = rcol[:, 0, bass.ds(h, 1)], rcol[:, 1, bass.ds(h, 1)], rcol[:, 2, bass.ds(h, 1)]
                        kk = rot[:r, t, 1, :, :].rearrange("p a b -> p (a b)")
                        dve.wait_ge(S["rot_done"], 2 * (h * NT + i + 1))
                    else:
                        winter, acol = cols[:r, t, 1, bass.ds(h, 1)], cols[:r, t, 3, bass.ds(h, 1)]
                        dcol = dec[:, h, t:t + 1] if t < NC else None
                        kk = pr[:r, t, K0:K0 + P]
                        dve.wait_ge(S["pj_out"], h * NT + i + 1)
                    if t < NC:
                        v.tensor_scalar(ka[:, :], kk, acol, SCALE, ALU.mult, ALU.mult).then_inc(S["ka_done"], 1)
                        dve.wait_ge(S["s_done"], h * NC + t + 1)
                        if not ret and t == 0:
                            dve.wait_ge(S["dm_done"], h + 1)
                        dmt = dm[:, h, :] if ret else dm[:, 0, t * P:(t + 1) * P]
                        v.scalar_tensor_tensor(sd[:, :], pS[:, 0:P], SCALE, dmt, ALU.mult,
                                               ALU.mult).then_inc(S["sd_done"], 1)
                        if t and ret and i + 1 < NT:
                            rotate(i + 1)
                        dve.wait_ge(S["a_done"], h * NC + t + 2)
                        dve.wait_ge(S["u_done"], h * NC + t + 1)
                        if t == 0:
                            v.tensor_copy(C[:, h, :], pU[:, 0:W]).then_inc(S["c_done"], 1)
                            ch.link(v.tensor_copy(hx[:, 0:W], pA[:, 0:W]))
                            if ret:
                                rotate(1)
                        else:
                            dve.wait_ge(S["c_done"], h * NC + t + 1)
                            v.scalar_tensor_tensor(C[:, h, :], C[:, h, :], dcol, pU[:, 0:W], ALU.mult,
                                                   ALU.add).then_inc(S["c_done"], 1)
                            ch.link(v.tensor_copy(hx[:, 0:W], pA[:, 0:W]))
                            ch.link(v.scalar_tensor_tensor(hx[:, 0:W], pA[:, 256:256 + W], winter, hx[:, 0:W],
                                                           ALU.mult, ALU.add))
                    else:
                        v.scalar_tensor_tensor(kbig[:, :, :], kk.unsqueeze(1).broadcast_to([NS, NS, P]),
                                               1.0 if ret else acol, dmask[:, :, :], ALU.mult,
                                               ALU.mult).then_inc(S["kb_done"], 1)
                        dve.wait_ge(S["cs_in"], 16)
                        for n in range(NS):
                            dn = rdec1[:, bass.ds(h, 1)] if ret else dec[:, h, NC + n:NC + n + 1]
                            dve.wait_ge(S["up_done"], h * NS + n + 1)
                            v.scalar_tensor_tensor(cs[:, h, n, :], cs[:, h, n, :], dn, (pU, pS)[n % 2][:, 0:W], ALU.mult,
                                                   ALU.add).then_inc(S["cs_done"], 1)
                        if ret:
                            rotate(i + 1)
                        dve.wait_ge(S["hs_done"], h + 2)
                        ch.link(v.tensor_copy(hx[:r, 0:W], pA[:r, 0:W]))
                    if not ret:
                        ch.link(v.tensor_scalar(den[:r, 0:1], hx[:r, P:P + 1], -1.0, cols[:r, t, 2, bass.ds(h, 1)],
                                                ALU.mult, ALU.max))
                        ch.link(v.tensor_tensor(den[:r, 0:1], den[:r, 0:1], hx[:r, P:P + 1], ALU.max))
                        ch.link(v.reciprocal(den[:r, 1:2], den[:r, 0:1]))
                        ch.link(v.tensor_scalar(hh[:r, t, :], hx[:r, 0:P], den[:r, 1:2], None, ALU.mult))
                    else:
                        ch.link(v.tensor_copy(hh[:r, t, :], hx[:r, 0:P]))
                    v.bn_stats(stats[:r, t, :], hh[:r, t, :]).then_inc(S["h_done"], 1)
                dve.wait_ge(S["h_done"], h * NT + NT + 1)
                ch.wait(ch.n)
                ch.mark(v.memset(den[:, 0:1], 1.0))
                for t in TOK:
                    ch.mark(v.bn_aggr(mv[:, t, :], stats[:, t, :]))
                ch.wait(ch.n)
                v.tensor_scalar(mv[:, :, 1], mv[:, :, 1], EPS, None, ALU.add).then_inc(S["var_done"], 1)
                dve.wait_ge(S["root_done"], h + 1)
                ch.link(v.reciprocal(mv[:, :, 1], mv[:, :, 1]))
                for t in TOK:
                    ch.mark(v.tensor_scalar(hh[:, t, :], hh[:, t, :], mv[:, t, 0:1], mv[:, t, 1:2], ALU.subtract,
                                            ALU.mult))
                ch.wait(ch.n)
                v.tensor_tensor(mix[:, :, bass.ds(g0 * P, P)], hh[:, :, :], gate[:, h % 2, :, :],
                                ALU.mult).then_inc(S["heads_done"], 1)
                dve.wait_ge(S["heads_done"], h + 3)
                ch.leave(H)


PER = {"mlstm": 72, "ret": 63, "select": 315, "decode": 13}


def routing_stages(nc, A, own, sb, ps, sem, ident, hnT, g_dram, g_tail):
    e1T = sb(own, "e1T", [P, T])
    e2T = sb(own, "e2T", [P, T])
    gtT = sb(own, "gtT", [P, T])
    with ExitStack() as both:
        idx = sb(both, "idx", [P, 4, NT, 2, 2, TOPK])
        tops = sb(both, "tops", [P, 4, NT, 2, TOPK])
        posn = sb(both, "posn", [P, 4, NT, 2, TOPK], U32)

        with ExitStack() as st, nc.Block() as block:
            wq = sb(st, "wq", [P, 2, ND, 2 * P])
            sk = sb(st, "sk", [P, PH, 2, NK])
            qT = sb(st, "qT", [P, 2, 2, T])
            tv = sb(st, "tv", [P, 4, 2, TOPK])
            ti = sb(st, "ti", [P, NT, 2, 2, TOPK], U32)
            rest = sb(st, "rest", [P, 4, 2, NK])
            cand = sb(st, "cand", [P, 4, TOPK * TOPK])
            crest = sb(st, "crest", [P, 4, TOPK * TOPK])
            ts_ = sb(st, "ts", [P, NT, 2, TOPK])
            tp_ = sb(st, "tp", [P, NT, 2, TOPK], U32)
            spare, carrier, zero1 = (sb(st, "spare" + x, [P, 1]) for x in "abc")
            pq = [ps(st, f"s_q{i}") for i in range(3)]
            pscore = [ps(st, f"s_s{i}", (P, 4, 2, NK)) for i in range(2)]
            wq_in = [sem(f"wq_in{i}") for i in range(2)]
            sk_in, q_done, q_out, score_done, score_used, zeroed, pair_done, chain = (
                sem(n) for n in ("sk_in", "q_done", "q_out", "score_done", "score_used", "s_zeroed", "pair_done", "s_chain"))
            TC = T // 3

            @block.sync
            def _(sp):
                sp.dma_start(sk[:, :, :, :], A["sub_keys"]).then_inc(sk_in, 16)
                for s in range(2):
                    sp.dma_start(wq[:, s, :, :], A["w_query"][s]).then_inc(wq_in[s], 16)
                for pr in range(3):
                    for s in range(2):
                        sp.wait_ge(q_done, 12 * pr + 6 * s + 6)
                        sp.dma_start(wq[:, s, :, :], A["w_query"][2 * pr + 2 + s]).then_inc(wq_in[s], 16)

            @block.tensor
            def _(pe):
                pe.sem_inc(score_done, 1)
                pe.wait_ge(sk_in, 16)
                with pe.Fori(0, 4) as pr:
                    for s in range(2):
                        pe.wait_ge(wq_in[s], 16 * pr + 16)
                        for side in range(2):
                            for c in range(3):
                                n = 6 * s + 3 * side + c
                                if n >= 3:
                                    pe.wait_ge(q_out, 12 * pr + n - 2)
                                for k in range(ND):
                                    last = nc.tensor.matmul(pq[c][:, 0:TC], wq[:, s, k, side * P:(side + 1) * P],
                                                            hnT[:, k, c * TC:(c + 1) * TC], start=(k == 0),
                                                            stop=(k == ND - 1))
                                last.then_inc(q_done, 1)
                        pe.wait_ge(q_out, 12 * pr + 6 * s + 6)
                        for gi, g in enumerate(GROUPS):
                            u = 3 * s + gi
                            if gi < 2:
                                pe.wait_ge(score_used, pr * 6 + u + 1)
                            for q, t in enumerate(g):
                                for side in range(2):
                                    if gi == 1 and q == len(g) - 1 and side == 1:
                                        pe.wait_ge(score_used, pr * 6 + u + 2)
                                    last = nc.tensor.matmul(pscore[u % 2][:rows(t), q, side, :],
                                                            qT[:, s, side, t * P:t * P + rows(t)],
                                                            sk[:, 2 * pr + s, side, :], start=True, stop=True)
                            last.then_inc(score_done, 1)

            @block.scalar
            def _(act):
                with act.Fori(0, 4) as pr:
                    for s in range(2):
                        for side in range(2):
                            for c in range(3):
                                n = 6 * s + 3 * side + c
                                act.wait_ge(q_done, 12 * pr + n + 1)
                                if side == 0 and c == 0:
                                    act.wait_ge(score_done, pr * 6 + 1)
                                nc.scalar.activation(qT[:, s, side, c * TC:(c + 1) * TC], pq[c][:, 0:TC],
                                                     ACT.Copy).then_inc(q_out, 1)

            @block.vector
            def _(dve):
                v = nc.vector
                ch = Chain(dve, chain)

                def tick():
                    ch.wait(ch.n)
                    ch.mark(v.tensor_copy(spare[:, :], zero1[:, :]))

                dve.sem_inc(score_used, 2)
                ch.link(v.memset(zero1[:, :], 0.0))
                ch.mark(v.memset(idx[:, :, :, :, :, :].rearrange("p a b c d e -> p (a b c d e)"), 0.0))
                ch.mark(v.memset(ti[:, :, :, :, :].rearrange("p a b c d -> p (a b c d)"), 0))
                ch.mark(v.memset(ts_[:, :, :, :].rearrange("p a b c -> p (a b c)"), 0.0))
                ch.link(v.memset(tp_[:, :, :, :].rearrange("p a b c -> p (a b c)"), 0))
                with dve.Fori(0, 4) as pr:
                    ch.enter(pr, PER["select"])
                    for s in range(2):
                        for gi, g in enumerate(GROUPS):
                            u, r, t0, G = 3 * s + gi, rows(g[0]), g[0], len(g)
                            both_sides = [(q, side) for q in range(G) for side in range(2)]
                            sc = pscore[u % 2]
                            dve.wait_ge(score_done, pr * 6 + u + 2)
                            ch.mark(v.tensor_copy(carrier[:, :], zero1[:, :]))
                            for q, side in both_sides:
                                ch.mark(v.max(tv[:r, q, side, 0:8], sc[:r, q, side, :]))
                            tick()
                            for q, side in both_sides:
                                ch.mark(v.max_index(ti[:r, t0 + q, s, side, 0:8], tv[:r, q, side, 0:8],
                                                    sc[:r, q, side, :]))
                                last = v.match_replace(rest[:r, q, side, :], tv[:r, q, side, 0:8],
                                                       sc[:r, q, side, :], LOW)
                                if (q, side) != both_sides[-1]:
                                    ch.mark(last)
                            last.then_inc(score_used, 1)
                            dve.wait_ge(score_used, pr * 6 + u + 3)
                            tick()
                            for q, side in both_sides:
                                ch.mark(v.max(tv[:r, q, side, 8:16], rest[:r, q, side, :]))
                            ch.wait(ch.n)
                            ch.mark(v.tensor_tensor(
                                cand[:r, 0:G, :].rearrange("p q (a b) -> p q a b", b=TOPK),
                                tv[:r, 0:G, 0, :].unsqueeze(3).broadcast_to([r, G, TOPK, TOPK]),
                                tv[:r, 0:G, 1, :].unsqueeze(2).broadcast_to([r, G, TOPK, TOPK]), ALU.add))
                            for q, side in both_sides:
                                ch.mark(v.max_index(ti[:r, t0 + q, s, side, 8:16], tv[:r, q, side, 8:16],
                                                    rest[:r, q, side, :]))
                            tick()
                            for q in range(G):
                                ch.mark(v.max(ts_[:r, t0 + q, s, 0:8], cand[:r, q, :]))
                            tick()
                            for q in range(G):
                                ch.mark(v.match_replace(crest[:r, q, :], ts_[:r, t0 + q, s, 0:8], cand[:r, q, :], LOW))
                                ch.mark(v.max_index(tp_[:r, t0 + q, s, 0:8], ts_[:r, t0 + q, s, 0:8], cand[:r, q, :]))
                            tick()
                            for q in range(G):
                                ch.mark(v.max(ts_[:r, t0 + q, s, 8:16], crest[:r, q, :]))
                            tick()
                            for q in range(G):
                                ch.mark(v.max_index(tp_[:r, t0 + q, s, 8:16], ts_[:r, t0 + q, s, 8:16], crest[:r, q, :]))
                    ch.wait(ch.n)
                    F = NT * 2 * TOPK
                    ch.mark(v.tensor_copy(idx[:, pr].rearrange("p t s i k -> p (t s i k)"),
                                          ti[:, :, :, :, :].rearrange("p t s i k -> p (t s i k)")))
                    ch.mark(v.tensor_copy(tops[:, pr].rearrange("p t s k -> p (t s k)"),
                                          ts_[:, :, :, :].rearrange("p t s k -> p (t s k)")))
                    ch.link(v.tensor_copy(posn[:, pr].rearrange("p t s k -> p (t s k)"),
                                          tp_[:, :, :, :].rearrange("p t s k -> p (t s k)")))
                    ch.leave(4)

        with ExitStack() as st, nc.Block() as block:
            K8 = PH * TOPK
            zero16 = sb(st, "zero16", [P, TOPK])
            i1 = sb(st, "d_i1", [P, PH, 2, TOPK])
            pu = sb(st, "d_pu", [P, K8], U32)
            ab_u = sb(st, "d_abu", [P, 2, K8], U32)
            ab = sb(st, "d_ab", [P, 2, K8])
            oh = sb(st, "d_oh", [P, K8, TOPK])
            se = sb(st, "d_se", [P, PH, TOPK])
            sm = sb(st, "d_sum", [P, PH, 2])
            e = sb(st, "d_e", [P, 3, K8])
            pt = [ps(st, f"d_t{i}") for i in range(2)]
            cst, diff_done, exp_done, e_done, t_done, t_out, chain = (
                sem(n) for n in ("d_const", "d_diff", "d_exp", "d_edone", "d_tdone", "d_tout", "d_chain"))

            @block.sync
            def _(sp):
                sp.dma_start(zero16[:, :], A["iota"][:, 0:TOPK]).then_inc(cst, 16)

            def tiles(eng, body):
                with eng.Fori(0, NC) as t:
                    body(t, P)
                body(NC, NS)

            @block.tensor
            def _(pe):
                def body(t, r):
                    pe.wait_ge(e_done, t + 1)
                    pe.wait_ge(t_out, t + 1)
                    for q in range(3):
                        last = nc.tensor.transpose(pt[0][:, q * P:q * P + r], e[:r, q, :], ident[:r, :r])
                    last.then_inc(t_done, 1)
                pe.sem_inc(t_done, 1)
                tiles(pe, body)

            @block.scalar
            def _(act):
                def body(t, r):
                    act.wait_ge(diff_done, t + 1)
                    nc.scalar.activation(se[:r, :, :], se[:r, :, :], ACT.Exp).then_inc(exp_done, 1)
                    act.wait_ge(t_done, t + 2)
                    for q, dst in enumerate((e1T, e2T, gtT)):
                        last = nc.scalar.activation(dst[:, bass.ds(t * P, r)], pt[0][:, q * P:q * P + r], ACT.Copy)
                    last.then_inc(t_out, 1)
                act.sem_inc(t_out, 1)
                tiles(act, body)

            @block.vector
            def _(dve):
                v = nc.vector
                ch = Chain(dve, chain)
                dve.wait_ge(cst, 16)

                def body(t, r):
                    ch.mark(v.tensor_copy(i1[:r, :, :, :].rearrange("p (a s) i k -> p a (s i k)", s=2),
                                          idx[:r, :, t, :, :, :].rearrange("p a s i k -> p a (s i k)")))
                    ch.link(v.tensor_copy(pu[:r, :].rearrange("p (a x) -> p a x", a=4),
                                          posn[:r, :, t, :, :].rearrange("p a s k -> p a (s k)")))
                    dve.wait_ge(t_done, t + 1)
                    for a in range(4):
                        last = v.tensor_tensor(se[:r, 2 * a:2 * a + 2, :], tops[:r, a, t, :, :],
                                               tops[:r, a, t, :, 0:1].broadcast_to([r, 2, TOPK]), ALU.subtract)
                    last.then_inc(diff_done, 1)
                    ch.mark(v.tensor_scalar(ab_u[:r, 0, :], pu[:r, :], 4, None, ALU.logical_shift_right))
                    ch.link(v.tensor_scalar(ab_u[:r, 1, :], pu[:r, :], TOPK - 1, None, ALU.bitwise_and))
                    ch.link(v.tensor_copy(ab[:r, :, :], ab_u[:r, :, :]))
                    for side in range(2):
                        ch.link(v.tensor_tensor(oh[:r, :, :], ab[:r, side, :].unsqueeze(2).broadcast_to([r, K8, TOPK]),
                                                zero16[:r, :].unsqueeze(1).broadcast_to([r, K8, TOPK]), ALU.is_equal))
                        oh4 = oh[:r, :, :].rearrange("p (h k) j -> p h k j", k=TOPK)
                        ch.link(v.tensor_tensor(oh4, oh4, i1[:r, :, side, :].unsqueeze(2).broadcast_to(
                            [r, PH, TOPK, TOPK]), ALU.mult))
                        ch.link(v.tensor_reduce(e[:r, side, :], oh[:r, :, :], AX.X, ALU.add))
                    dve.wait_ge(exp_done, t + 1)
                    ch.link(v.tensor_reduce(sm[:r, :, 0], se[:r, :, :], AX.X, ALU.add))
                    ch.link(v.reciprocal(sm[:r, :, 1], sm[:r, :, 0]))
                    v.tensor_tensor(e[:r, 2, :].rearrange("p (h k) -> p h k", k=TOPK), se[:r, :, :],
                                    sm[:r, :, 1:2].broadcast_to([r, PH, TOPK]), ALU.mult).then_inc(e_done, 1)
                    dve.wait_ge(e_done, t + 1)

                with dve.Fori(0, NC) as t:
                    ch.enter(t, PER["decode"])
                    body(t, P)
                    ch.leave(NC)
                body(NC, NS)

    with ExitStack() as st, nc.Block() as block:
        STEP, HALF = 8, 4
        iota = sb(st, "iota", [P, NK])
        one1 = sb(st, "one1", [P, STEP, NK])
        one2 = sb(st, "one2", [P, STEP, NK])
        gbuf = sb(st, "gbuf", [P, 2, NK, SUB])
        pg = [ps(st, f"g_p{i}") for i in range(2)]
        cst, slot_free, hot_done, bank_full, bank_out = (
            sem(n) for n in ("g_const", "g_slot_free", "g_hot", "g_full", "g_bank_out"))
        saved = [sem(f"g_saved{i}") for i in range(2)]

        @block.sync
        def _(sp):
            for s in range(2):
                sp.sem_inc(saved[s], 16)
            sp.dma_start(iota[:, :], A["iota"]).then_inc(cst, 16)
            with sp.Fori(0, NSUB // 2) as j:
                for s in range(2):
                    sp.wait_ge(bank_out, 32 * j + 16 * s + 18)
                    sp.dma_start(g_dram[2 * j + s], gbuf[:, s, :, :]).then_inc(saved[s], 16)
            for s in range(2):
                sp.wait_ge(saved[s], 16 * (NSUB // 2) + 16)

        @block.vector
        def _(dve):
            v = nc.vector
            dve.wait_ge(cst, 16)

            def step(i):
                for k in range(STEP):
                    tok = bass.ds(i * STEP + k, 1)
                    dve.wait_ge(slot_free, i * STEP + k + 1)
                    v.tensor_scalar(one1[:, k, :], iota[:, :], e1T[:, tok], None, ALU.is_equal)
                    v.tensor_scalar(one2[:, k, :], iota[:, :], e2T[:, tok], gtT[:, tok], ALU.is_equal,
                                    ALU.mult).then_inc(hot_done, 1)
            with dve.Fori(0, SEQ // STEP) as i:
                step(i)
            step(SEQ // STEP)

        @block.tensor
        def _(pe):
            pe.sem_inc(slot_free, STEP)

            def step(i):
                for k in range(STEP):
                    if k % HALF == 0:
                        pe.wait_ge(bank_out, 2 * i + k // HALF + 1)
                    pe.wait_ge(hot_done, i * STEP + k + 1)
                    last = nc.tensor.matmul(pg[k // HALF][:, (k % HALF) * NK:(k % HALF + 1) * NK], one2[:, k, :],
                                            one1[:, k, :], start=True, stop=True)
                    last.then_inc(slot_free, 1)
            with pe.Fori(0, SEQ // STEP) as i:
                step(i)
            step(SEQ // STEP)

        @block.scalar
        def _(act):
            act.sem_inc(bank_out, 2)

            def out(i, b, dst):
                act.wait_ge(slot_free, STEP * i + STEP + HALF * (b + 1))
                nc.scalar.activation(dst, pg[b][:, :].rearrange("p (t i) -> p i t", t=HALF),
                                     ACT.Copy).then_inc(bank_out, 1)
            with act.Fori(0, NSUB // 2) as j:
                for s in range(2):
                    act.wait_ge(saved[s], 16 * j + 16)
                    with act.Fori(0, SUB // STEP) as i:
                        for b in range(2):
                            out((2 * j + s) * (SUB // STEP) + i, b, gbuf[:, s, :, bass.ds(i * STEP + b * HALF, HALF)])
            for b in range(2):
                out(SEQ // STEP, b, g_tail[:, :, b * HALF:(b + 1) * HALF])


def expert_sweep(nc, A, O, own, sb, ps, sem, ident, hnT, g_dram, g_tail, x2_dram, group):
    n0 = f"x{group}_"
    t0 = group * 512
    TG = 512 if group == 0 else T - 512
    CH = -(-TG // 512)
    C = TG // CH
    NV = 4 // CH
    SG = 512 // SUB
    NP = NK // 2
    acc = sb(own, n0 + "acc", [P, ND, TG])

    with ExitStack() as st, nc.Block() as block:
        hn_hi, hn_lo = (sb(st, n0 + "hn" + x, [P, ND, TG], F32R) for x in ("h", "l"))
        u_raw = sb(st, n0 + "uraw", [P, 2, 2, ND, P])
        v_raw = sb(st, n0 + "vraw", [P, 2, 2, D])
        g_raw = sb(st, n0 + "graw", [P, 2, SG, 2, SUB])
        u_hi, u_lo = (sb(st, n0 + "u" + x, [P, 2, ND, P], F32R) for x in ("h", "l"))
        v_hi, v_lo = (sb(st, n0 + "v" + x, [P, 2, 2, D], F32R) for x in ("h", "l"))
        w_hi, w_lo = (sb(st, n0 + "w" + x, [P, 2, 2, TG], F32R) for x in ("h", "l"))
        gel = sb(st, n0 + "gel", [P, 2, TG])
        wf = sb(st, n0 + "wf", [P, 2, TG])
        pa = [ps(st, f"{n0}pa{i}", (P, CH, 512)) for i in range(2)]
        pv = [ps(st, f"{n0}pv{i}", (P, CH, 512)) for i in range(NV)]
        u_in, v_in, g_in = ([sem(f"x_{x}_in{i}") for i in range(2)] for x in "uvg")
        hn_hi_done, hn_lo_done, uhi_done, ulo_done, vhi_done, vlo_done, a_done, gelu_done, wf_done, whi_done, \
            wlo_done, vmm_done, acc_done = (
                sem("x_" + n) for n in ("hnhi", "hnlo", "uhi", "ulo", "vhi", "vlo", "adone", "gelu", "wf", "whi",
                                      "wlo", "vmm", "accd"))

        def steps(eng, body):
            body(0, 0, True, False)
            with eng.Fori(0, NP // 2 - 1) as j:
                body(2 * j + 1, 1, False, False)
                body(2 * j + 2, 0, False, False)
            body(NP - 1, 1, False, True)

        @block.sync
        def _(sp):
            def load(g, s):
                sp.dma_start(u_raw[:, s], A["peer_u"][g]).then_inc(u_in[s], 16)
                sp.dma_start(g_raw[:, s].rearrange("p c e t -> p c (e t)"),
                             g_dram[group * SG:(group + 1) * SG, :, bass.ds(2 * g, 2), :].rearrange(
                                 "c i e t -> i c (e t)")).then_inc(g_in[s], 16)
                sp.dma_start(v_raw[:, s], A["peer_v"][g]).then_inc(v_in[s], 16)
            for s in range(2):
                load(s, s)
            with sp.Fori(0, NP // 2 - 1) as j:
                for s in range(2):
                    g = 2 * j + s
                    sp.wait_ge(ulo_done, 2 * g + 2)
                    sp.wait_ge(wf_done, 2 * g + 2)
                    sp.wait_ge(vlo_done, 2 * g + 2)
                    load(g + 2, s)

        @block.tensor
        def _(pe):
            mm = nc.tensor.matmul

            def up(g, e):
                n = 2 * g + e
                pe.wait_ge(ulo_done, n + 1)
                for c in range(CH):
                    s = slice(c * C, (c + 1) * C)
                    for k in range(ND):
                        mm(pa[e][:, c, 0:C], u_hi[:, e, k, :], hn_hi[:, k, s], start=(k == 0), stop=False)
                        mm(pa[e][:, c, 0:C], u_hi[:, e, k, :], hn_lo[:, k, s], start=False, stop=False)
                        last = mm(pa[e][:, c, 0:C], u_lo[:, e, k, :], hn_hi[:, k, s], start=False,
                                  stop=(k == ND - 1))
                last.then_inc(a_done, 1)

            def down(g, s):
                pe.wait_ge(wlo_done, 2 * g + 2)
                pe.wait_ge(vlo_done, 2 * g + 2)
                for b in range(ND):
                    pe.wait_ge(acc_done, ND * g + b + 1)
                    d = slice(b * P, (b + 1) * P)
                    for c in range(CH):
                        t = slice(c * C, (c + 1) * C)
                        for e in range(2):
                            mm(pv[b % NV][:, c, 0:C], v_hi[:, s, e, d], w_hi[:, s, e, t], start=(e == 0), stop=False)
                            mm(pv[b % NV][:, c, 0:C], v_hi[:, s, e, d], w_lo[:, s, e, t], start=False, stop=False)
                            last = mm(pv[b % NV][:, c, 0:C], v_lo[:, s, e, d], w_hi[:, s, e, t], start=False,
                                      stop=(e == 1))
                    last.then_inc(vmm_done, 1)

            def body(g, s, first, last):
                for e in range(2):
                    if not first:
                        pe.wait_ge(gelu_done, 2 * g + e - 1)
                    up(g, e)
                if not first:
                    down(g - 1, 1 - s)

            pe.sem_inc(vmm_done, 1)
            pe.wait_ge(hn_lo_done, ND)
            steps(pe, body)
            down(NP - 1, 1)

        @block.scalar
        def _(act):
            def cp(dst, src):
                return nc.scalar.activation(dst, src, ACT.Copy)

            for k in range(ND):
                cp(hn_hi[:, k, :], hnT[:, k, t0:t0 + TG]).then_inc(hn_hi_done, 1)
            for e in range(2):
                act.wait_ge(u_in[0], 16)
                cp(u_hi[:, e], u_raw[:, 0, e]).then_inc(uhi_done, 1)

            def body(g, s, first, last):
                passes = loads_of(g, s)
                for e in range(2):
                    n = 2 * g + e
                    act.wait_ge(a_done, n + 1)
                    if not first:
                        act.wait_ge(wf_done, n - 1)
                    nc.scalar.activation(gel[:, e, :].rearrange("p (c t) -> p c t", c=CH), pa[e][:, :, 0:C],
                                         ACT.Gelu).then_inc(gelu_done, 1)
                    if not last:
                        act.wait_ge(u_in[1 - s], 16 * loads_of(g + 1, 1 - s))
                        cp(u_hi[:, e], u_raw[:, 1 - s, e]).then_inc(uhi_done, 1)
                    if e == 0 and not first:
                        act.wait_ge(vmm_done, ND * (g - 1) + 1)
                    act.wait_ge(v_in[s], 16 * passes)
                    cp(v_hi[:, s, e, :], v_raw[:, s, e, :]).then_inc(vhi_done, 1)
                    act.wait_ge(wf_done, n + 1)
                    cp(w_hi[:, s, e, :], wf[:, e, :]).then_inc(whi_done, 1)
            steps(act, body)

        @block.vector
        def _(dve):
            v = nc.vector

            def lo(dst, src, hi):
                return v.tensor_tensor(dst, src, hi.bitcast(F32), ALU.subtract)

            v.memset(acc[:, :, :], 0.0).then_inc(acc_done, NV)
            for k in range(ND):
                dve.wait_ge(hn_hi_done, k + 1)
                lo(hn_lo[:, k, :], hnT[:, k, t0:t0 + TG], hn_hi[:, k, :]).then_inc(hn_lo_done, 1)
            for e in range(2):
                dve.wait_ge(uhi_done, e + 1)
                lo(u_lo[:, e], u_raw[:, 0, e], u_hi[:, e]).then_inc(ulo_done, 1)

            def add(g, blocks):
                for b in blocks:
                    if b == 0:
                        dve.wait_ge(acc_done, NV + ND * g)
                    dve.wait_ge(vmm_done, ND * g + b + 2)
                    a3 = acc[:, b, :].rearrange("p (c t) -> p c t", c=CH)
                    v.tensor_tensor(a3, a3, pv[b % NV][:, :, 0:C], ALU.add).then_inc(acc_done, 1)

            def body(g, s, first, last):
                passes = loads_of(g, s)

                def sums(e, part):
                    if e == 1 and not first:
                        add(g - 1, (2 * part, 2 * part + 1))

                for e in range(2):
                    n = 2 * g + e
                    sums(e, 0)
                    if not last:
                        dve.wait_ge(uhi_done, n + 3)
                        lo(u_lo[:, e], u_raw[:, 1 - s, e], u_hi[:, e]).then_inc(ulo_done, 1)
                    sums(e, 1)
                    dve.wait_ge(gelu_done, n + 1)
                    dve.wait_ge(g_in[s], 16 * passes)
                    if not first:
                        dve.wait_ge(whi_done, n - 1)
                        dve.wait_ge(wlo_done, n - 1)
                    mul = v.tensor_tensor(wf[:, e, 0:512].rearrange("p (c t) -> p c t", c=SG),
                                          gel[:, e, 0:512].rearrange("p (c t) -> p c t", c=SG), g_raw[:, s, :, e, :],
                                          ALU.mult)
                    if group:
                        mul = v.tensor_tensor(wf[:, e, 512:TG], gel[:, e, 512:TG], g_tail[:, n, :], ALU.mult)
                    mul.then_inc(wf_done, 1)
                    sums(e, 2)
                    dve.wait_ge(vhi_done, n + 1)
                    lo(v_lo[:, s, e, :], v_raw[:, s, e, :], v_hi[:, s, e, :]).then_inc(vlo_done, 1)
                    sums(e, 3)
                    dve.wait_ge(whi_done, n + 1)
                    lo(w_lo[:, s, e, :], wf[:, e, :], w_hi[:, s, e, :]).then_inc(wlo_done, 1)
            steps(dve, body)
            add(NP - 1, range(ND))

    TL = range(4) if group == 0 else range(4, NT)
    with ExitStack() as st, nc.Block() as block:
        x2 = sb(st, n0 + "x2", [P, NT, D])
        gf = sb(st, n0 + "gf", [P, D])
        junk = sb(st, n0 + "junk", [P, D])
        ss = sb(st, n0 + "ss", [P, NT])
        rstd = sb(st, n0 + "rstd", [P, NT])
        pt = [ps(st, f"{n0}pt{i}") for i in range(4)]
        x_in = sem("x_e_xin")
        g_in2, ones_set, tr_done, x_done, sq_done, ms_done, root_done, rstd_done, xs_done, y_done, y_out = (
            sem("x_e_" + n) for n in ("g", "ones", "tr", "x", "sq", "ms", "root", "rstd", "xs", "y", "out"))

        @block.sync
        def _(sp):
            sp.dma_start(gf[:, :], A["g_final"]).then_inc(g_in2, 16)
            for t in TL:
                sp.dma_start(x2[:rows(t), t, :], x2_dram[t * P:t * P + rows(t), :]).then_inc(x_in, 16)
            for i, t in enumerate(TL):
                sp.wait_ge(y_done, i + 1)
                sp.dma_start(O["y"][t * P:t * P + rows(t), :], x2[:rows(t), t, :]).then_inc(y_out, 16)
            sp.wait_ge(y_out, 16 * len(TL))

        @block.tensor
        def _(pe):
            for i, t in enumerate(TL):
                for n in range(2):
                    u = 2 * i + n
                    if u >= 4:
                        pe.wait_ge(x_done, u - 3)
                    for k in range(4):
                        last = nc.tensor.transpose(pt[u % 4][:rows(t), k * P:(k + 1) * P],
                                                   acc[:, 4 * n + k, t * P - t0:t * P - t0 + rows(t)], ident[:, :])
                    last.then_inc(tr_done, 1)

        @block.scalar
        def _(act):
            act.wait_ge(ones_set, 1)
            for i, t in enumerate(TL):
                act.wait_ge(x_done, 2 * i + 2)
                if i:
                    act.wait_ge(sq_done, i)
                nc.scalar.activation(junk[:rows(t), :], x2[:rows(t), t, :], ACT.Square,
                                     accum_out=ss[:rows(t), t:t + 1]).then_inc(sq_done, 1)
            act.wait_ge(ms_done, 1)
            nc.scalar.activation(rstd[:, :], ss[:, :], ACT.Sqrt).then_inc(root_done, 1)

        @block.vector
        def _(dve):
            nc.vector.memset(ss[:, :], 1.0).then_inc(ones_set, 1)
            dve.wait_ge(x_in, 16 * len(TL))
            for i, t in enumerate(TL):
                for n in range(2):
                    u = 2 * i + n
                    s = slice(n * 512, (n + 1) * 512)
                    dve.wait_ge(tr_done, u + 1)
                    nc.vector.tensor_tensor(x2[:rows(t), t, s], pt[u % 4][:rows(t), :], x2[:rows(t), t, s],
                                            ALU.add).then_inc(x_done, 1)
            dve.wait_ge(sq_done, len(TL))
            nc.vector.tensor_scalar(ss[:, :], ss[:, :], 1.0 / D, EPS, ALU.mult, ALU.add).then_inc(ms_done, 1)
            dve.wait_ge(root_done, 1)
            nc.vector.reciprocal(rstd[:, :], rstd[:, :]).then_inc(rstd_done, 1)
            dve.wait_ge(rstd_done, 1)
            dve.wait_ge(g_in2, 16)
            for i, t in enumerate(TL):
                nc.vector.scalar_tensor_tensor(x2[:rows(t), t, :], x2[:rows(t), t, :], rstd[:rows(t), t:t + 1],
                                               gf[:rows(t), :], ALU.mult, ALU.mult).then_inc(y_done, 1)


def loads_of(g, s):
    return g // 2 + 1


def constants():
    f = np.float32
    j, t = np.arange(P)[:, None], np.arange(P)[None, :]
    lg = np.log1p(-np.power(2.0, -5.0 - np.arange(H)))
    dmat = np.stack([np.where(j <= t, np.exp(np.maximum(t - j, 0) * g), 0.0) for g in lg], axis=1)
    idx = np.arange(P)[:, None]
    rcol = np.stack([np.exp((idx + 1) * lg), np.exp((P - 1 - idx) * lg), np.exp(P * lg) + 0 * idx], axis=1)
    inv = np.power(f(10000.0), -np.arange(P // 2, dtype=f) * f(2.0 / P)).astype(f)
    ang = (np.arange(SEQ, dtype=f)[:, None] * inv).astype(f).astype(np.float64)
    cosin = np.stack([np.cos(ang), np.sin(ang)]).reshape(2, NC, P, P // 2).transpose(2, 0, 1, 3)
    start = np.ones((H, T))
    start[:, 0:SEQ:P] = 0
    start[:, SEQ:] = 0
    c = {
        "ident": np.eye(P),
        "iota": np.broadcast_to(np.arange(P), (P, P)),
        "start_mask": start,
        "delta4": np.eye(H),
        "ones4": np.ones((H, P)),
        "neg": np.where(j <= t, 0.0, NEG),
        "dmask": np.broadcast_to((np.eye(NS) * SCALE)[:, :, None], (NS, NS, P)),
        "dmat": dmat,
        "cosin": cosin,
        "rcol": rcol,
        "rdec1": np.broadcast_to(np.exp(lg), (P, H)),
        "inv": np.broadcast_to(inv, (NS, P // 2)),
    }
    return {k: np.ascontiguousarray(v, dtype=f) for k, v in c.items()}


def lay_out(x_prompt, x_sample, state_mlstm_C, state_mlstm_n, state_mlstm_m, state_ret_S, pos_sample,
            rms_mix_g, w_in, b_igate, b_fgate, norm_mlstm_g, norm_ret_g, w_out, rms_ffn_g,
            w_query, sub_keys, peer_u, peer_v, rms_final_g):
    def by_block(m):
        return m.reshape(-1, P, m.shape[-1]).transpose(1, 0, 2)

    w = w_in[0]
    HP = H * P
    off_i, off_r = 4 * HP, 4 * HP + 2 * H
    heads = [by_block(np.concatenate([w[:, o + s * HP + h * P:o + s * HP + (h + 1) * P] for s in range(4)], axis=1))
             for o in (0, off_r) for h in range(H)]
    gains = np.stack([g.reshape(ND, P).T for g in (rms_mix_g[0], np.concatenate([norm_mlstm_g[0], norm_ret_g[0]]),
                                                   rms_ffn_g[0], rms_final_g)], axis=1)
    cn = np.concatenate([state_mlstm_C[0], state_mlstm_n[0][..., None]], axis=-1)
    return {
        "x": np.concatenate([x_prompt[0], x_sample[:, 0]]),
        "gains": gains,
        "w_heads": np.stack(heads),
        "w_if": by_block(w[:, off_i:off_r]),
        "b_if": np.stack([b_igate[0], b_fgate[0]], axis=1),
        "m_in": state_mlstm_m[0].T,
        "csm": cn.transpose(2, 1, 0, 3),
        "csr": state_ret_S[0].transpose(2, 1, 0, 3),
        "pos": pos_sample.reshape(NS, 1),
        "w_out": by_block(w_out[0]),
        "w_query": by_block(w_query[0]).reshape(P, ND, PH, 2 * P).transpose(2, 0, 1, 3),
        "sub_keys": sub_keys[0].transpose(3, 0, 1, 2),
        "peer_u": peer_u[0].reshape(NK // 2, 2, P, ND, P).transpose(0, 4, 1, 3, 2),
        "peer_v": peer_v[0].reshape(NK // 2, 2, P, D).transpose(0, 2, 1, 3),
        "g_final": np.broadcast_to(rms_final_g, (P, D)),
    }


OUTPUTS = {"y": (T, D), "cm": (H, P, P + 1), "csm": (H, P, NS, P + 1), "m": (H, 1 + NS), "cr": (H, P, P), "csr": (H, P, NS, P)}


def kernel(**inputs):
    import concourse.bacc as bacc
    from concourse.bass_utils import run_bass_kernel_spmd

    nc = bacc.Bacc("TRN2", target_bir_lowering=False, num_devices=1)
    arrays = {**lay_out(**{k: np.asarray(v) for k, v in inputs.items()}), **constants()}
    arrays = {f"in_{k}": np.ascontiguousarray(v) for k, v in arrays.items()}
    A = {k[3:]: nc.dram_tensor(k, v.shape, mybir.dt.from_np(v.dtype), kind="ExternalInput").ap()
         for k, v in arrays.items()}
    O = {k: nc.dram_tensor(f"out_{k}", s, F32, kind="ExternalOutput").ap() for k, s in OUTPUTS.items()}
    build(nc, A, O)
    got = run_bass_kernel_spmd(nc, [arrays], core_ids=[0]).results[0]
    y, cm, csm, m, cr, csr = (np.asarray(got[f"out_{k}"]) for k in ("y", "cm", "csm", "m", "cr", "csr"))
    csm = csm.transpose(2, 0, 1, 3)
    out = (y[None, :SEQ], y[SEQ:, None], cm[None, None, ..., :P], cm[None, None, ..., P], m[:, 0].reshape(1, 1, H),
           cr[None, None], csm[None, ..., :P], csm[None, ..., P], m[:, 1:].T[None], csr.transpose(2, 0, 1, 3)[None])
    return tuple(np.ascontiguousarray(o) for o in out)
```

```python
from contextlib import ExitStack

import numpy as np
import concourse.bass as bass
from concourse import mybir

F32 = mybir.dt.float32
F32R = mybir.dt.float32r
U32 = mybir.dt.uint32
I32 = mybir.dt.int32
ALU = mybir.AluOpType
ACT = mybir.ActivationFunctionType
AX = mybir.AxisListType

P = 128
D = 1024
ND = D // P
SEQ = 1024
NC = SEQ // P
NS = 8
T = SEQ + NS
NT = NC + 1
H = 4
EPS = 1e-6
SCALE = float(P) ** -0.5
PH, NK, TOPK = 8, 128, 16
GROUPS = [range(0, 4), range(4, NC), range(NC, NT)]
SUB = 64
NSUB = SEQ // SUB
LOW = -3.0e38
PROJ = 3 * P + 8
K0, V0 = P, 2 * P
NEG = -1.0e30


def rows(t):
    return P if t < NC else NS


class Chain:

    def __init__(self, eng, sem, start=0):
        self.eng, self.sem, self.n, self.start = eng, sem, 0, start
        self.loop, self.per = None, 0

    def enter(self, i, per):
        self.start += self.n
        self.loop, self.per, self.n = i, per, 0

    def leave(self, passes):
        assert self.n == self.per, (self.n, self.per)
        self.start += self.per * passes
        self.loop, self.n = None, 0

    def value(self, n=None):
        n = self.n if n is None else n
        return self.start + n if self.loop is None else self.loop * self.per + (self.start + n)

    def link(self, ins):
        ins.then_inc(self.sem, 1)
        self.n += 1
        self.wait(self.n)
        return self.n

    def mark(self, ins):
        ins.then_inc(self.sem, 1)
        self.n += 1
        return self.n

    def wait(self, n):
        self.eng.wait_ge(self.sem, self.value(n))


UNITS = [(dk, g) for g in range(2) for dk in range(ND)] + [(0, 2)]


def transpose_units_pe(nc, pe, src, ident, bank, tr_done, tr_free, ready):
    for u, (dk, g) in enumerate(UNITS):
        if dk == 0:
            ready(g)
        if u >= len(bank):
            pe.wait_ge(tr_free, u - len(bank) + 1)
        b = bank[u % len(bank)]
        if g < 2:
            for k in range(4):
                t = 4 * g + k
                last = nc.tensor.transpose(b[:, k * P:(k + 1) * P], src[:, t, dk * P:(dk + 1) * P], ident[:, :])
        else:
            for k in range(ND):
                last = nc.tensor.transpose(b[:, k * NS:(k + 1) * NS], src[:NS, NC, k * P:(k + 1) * P],
                                           ident[:NS, :NS])
        last.then_inc(tr_done, 1)


def transpose_units_out(nc, dve, dst, gcol, bank, tr_done, tr_free):
    for u, (dk, g) in enumerate(UNITS):
        dve.wait_ge(tr_done, u + 1)
        b = bank[u % len(bank)]
        if g < 2:
            nc.vector.tensor_scalar(dst[:, dk, 4 * g * P:(4 * g + 4) * P], b[:, :], gcol[:, dk:dk + 1], None,
                                    ALU.mult).then_inc(tr_free, 1)
        else:
            nc.vector.tensor_tensor(dst[:, :, SEQ:T], b[:, 0:ND * NS].rearrange("p (k n) -> p k n", k=ND),
                                    gcol[:, :].unsqueeze(2).broadcast_to([P, ND, NS]),
                                    ALU.mult).then_inc(tr_free, 1)


def build(nc, A, O):
    with ExitStack() as top:
        def sb(ctx, name, shape, dt=F32):
            return ctx.enter_context(nc.sbuf_tensor(name, shape, dt))

        def ps(ctx, name, shape=(P, 512), dt=F32):
            return ctx.enter_context(nc.psum_tensor(name, list(shape), dt))

        held = {}

        def sem(name):
            if name not in held:
                held[name] = top.enter_context(nc.semaphore(name))
            return held[name]

        def clear(prefix):
            with nc.Block() as block:
                @block.vector
                def _(dve):
                    for name in held:
                        if name.startswith(prefix):
                            dve.sem_clear(held[name])

        x2_dram = nc.dram_tensor("x2_scratch", (T, D), F32, kind="Internal").ap()
        g_dram = nc.dram_tensor("gate_scratch", (NSUB, NK, NK, SUB), F32, kind="Internal").ap()

        ident = sb(top, "ident", [P, P])
        x2_saved = sem("x2_saved")
        hnT = sb(top, "hnT", [P, ND, T])
        g_tail = sb(top, "g_tail", [NK, NK, NS])
        with ExitStack() as mixer:
            mixer_stages(nc, A, O, mixer, sb, ps, sem, clear, ident, hnT, x2_dram, x2_saved)
        u_raw = sb(top, "u_raw", [P, 2, 2, ND, P])
        v_raw = sb(top, "v_raw", [P, 2, 2, D])
        u_in, v_in = ([sem(f"{x}_in{i}") for i in range(2)] for x in "uv")

        def load_rows(sp, g, s):
            sp.dma_start(u_raw[:, s], A["peer_u"][g]).then_inc(u_in[s], 16)
            sp.dma_start(v_raw[:, s], A["peer_v"][g]).then_inc(v_in[s], 16)

        with ExitStack() as routing:
            routing_stages(nc, A, routing, sb, ps, sem, ident, hnT, g_dram, g_tail, load_rows)
        for group in range(2):
            if group:
                clear("x_")
            with ExitStack() as sweep:
                expert_sweep(nc, A, O, sweep, sb, ps, sem, ident, hnT, g_dram, g_tail, x2_dram, group,
                             u_raw, v_raw, u_in, v_in, load_rows)


def mixer_stages(nc, A, O, own, sb, ps, sem, clear, ident, hnT, x2_dram, x2_saved):
    mix = sb(own, "mix", [P, NT, D])
    xnT = hnT
    gain = sb(own, "gain", [P, 4, ND])
    cols = sb(own, "cols", [P, NT, 4, H])
    dec = sb(own, "dec", [P, H, 2 * NC])
    heads = own.enter_context(ExitStack())
    negmd = sb(heads, "negmd", [H, H, SEQ])
    w = sb(heads, "w_heads", [P, 2, ND, 512])
    w_in = [sem(f"w_in{s}") for s in range(2)]
    gmix, gnm, gffn = gain[:, 0, :], gain[:, 1, :], gain[:, 2, :]

    with ExitStack() as st, nc.Block() as block:
        junk = sb(st, "sq_junk", [P, D])
        ss = sb(st, "ss", [P, NT])
        rstd = sb(st, "rstd", [P, NT])
        xn = sb(st, "xn", [P, NT, D])
        bank = [ps(st, f"n_tr{i}") for i in range(4)]
        x_in = [sem(f"x_in{t}") for t in range(NT)]
        const_in, ones_set, sq_done, ms_done, root_done, rstd_done, xn_done, tr_done, tr_free = (
            sem(n) for n in ("const_in", "ones_set", "sq_done", "ms_done", "root_done", "rstd_done", "xn_done",
                             "n_tr_done", "n_tr_free"))

        @block.sync
        def _(sp):
            for t in range(NT):
                sp.dma_start(mix[:rows(t), t, :], A["x"][t * P:t * P + rows(t), :]).then_inc(x_in[t], 16)
            sp.dma_start(ident[:, :], A["ident"]).then_inc(const_in, 16)
            sp.dma_start(gain[:, :, :], A["gains"]).then_inc(const_in, 16)
            sp.sem_inc(w_in[1], 16)
            for s in range(2):
                sp.dma_start(w[:, s, :, :], A["w_heads"][s]).then_inc(w_in[s], 16)

        @block.scalar
        def _(act):
            act.wait_ge(ones_set, 1)
            for t in range(NT):
                act.wait_ge(x_in[t], 16)
                if t:
                    act.wait_ge(sq_done, t)
                nc.scalar.activation(junk[:rows(t), :], mix[:rows(t), t, :], ACT.Square,
                                     accum_out=ss[:rows(t), t:t + 1]).then_inc(sq_done, 1)
            act.wait_ge(ms_done, 1)
            nc.scalar.activation(rstd[:, :], ss[:, :], ACT.Sqrt).then_inc(root_done, 1)
            act.wait_ge(rstd_done, 1)
            for t in range(NT):
                nc.scalar.activation(xn[:rows(t), t, :], mix[:rows(t), t, :], ACT.Copy,
                                     scale=rstd[:rows(t), t:t + 1]).then_inc(xn_done, 1)

        @block.vector
        def _(dve):
            nc.vector.memset(ss[:, :], 1.0).then_inc(ones_set, 1)
            dve.wait_ge(sq_done, NT)
            nc.vector.tensor_scalar(ss[:, :], ss[:, :], 1.0 / D, EPS, ALU.mult, ALU.add).then_inc(ms_done, 1)
            dve.wait_ge(root_done, 1)
            nc.vector.reciprocal(rstd[:, :], rstd[:, :]).then_inc(rstd_done, 1)
            dve.wait_ge(const_in, 32)
            transpose_units_out(nc, dve, xnT, gmix, bank, tr_done, tr_free)

        @block.tensor
        def _(pe):
            pe.wait_ge(const_in, 32)
            transpose_units_pe(nc, pe, xn, ident, bank, tr_done, tr_free,
                               lambda g: pe.wait_ge(xn_done, (4, 8, NT)[g]))

    with ExitStack() as st, nc.Block() as block:
        wif = sb(st, "wif", [P, ND, 2 * H])
        bif = sb(st, "bif", [H, 2])
        msk = sb(st, "chunk_start_mask", [H, T])
        delta = sb(st, "delta4", [H, H])
        ones4 = sb(st, "ones4a", [H, P])
        m_in = sb(st, "m_in", [H, NS])
        ig = sb(st, "ig", [H, T])
        zf = sb(st, "zf", [H, T])
        ez = sb(st, "ez", [H, T])
        lf = sb(st, "lf", [H, T])
        b = sb(st, "b", [H, T])
        shift = sb(st, "shift", [H, SEQ])
        M = sb(st, "M", [H, T])
        row = sb(st, "row", [H, 4, T])
        mnew = sb(st, "mnew", [H, NC + NS])
        mprev = sb(st, "mprev", [H, NC])
        decmd = sb(st, "decmd", [H, H, 2 * NC])
        pi = [ps(st, f"g_i{i}") for i in range(3)]
        pf = [ps(st, f"g_f{i}") for i in range(3)]
        pc, pd = ps(st, "g_cols"), ps(st, "g_dec")
        gate_in, pre_done, z_done, e1_done, e2_done, rows_done, cols_ps, cols_out, dec_ps, exp_out, m_out, chain = (
            sem(n) for n in ("gate_in", "gate_pre", "gate_z", "gate_exp", "gate_ln", "gate_rows", "cols_ps",
                             "cols_out", "dec_ps", "cols_exp", "m_out", "gate_chain"))
        TC = T // 3

        @block.sync
        def _(sp):
            for dst, src in ((wif[:, :, :], A["w_if"]), (bif[:, :], A["b_if"]), (msk[:, :], A["start_mask"]),
                             (delta[:, :], A["delta4"]), (m_in[:, :], A["m_in"]), (ones4[:, :], A["ones4"])):
                sp.dma_start(dst, src).then_inc(gate_in, 16)
            sp.wait_ge(rows_done, 1)
            sp.dma_start(O["m"], mnew[:, NC - 1:NC + NS]).then_inc(m_out, 16)
            sp.wait_ge(m_out, 16)

        @block.tensor
        def _(pe):
            pe.wait_ge(gate_in, 96)
            for c in range(3):
                for g, bk in ((0, pi), (1, pf)):
                    for k in range(ND):
                        last = nc.tensor.matmul(bk[c][:H, 0:TC], wif[:, k, g * H:(g + 1) * H],
                                                xnT[:, k, c * TC:(c + 1) * TC], start=(k == 0), stop=(k == ND - 1))
            last.then_inc(pre_done, 1)
            pe.wait_ge(rows_done, 1)
            for t in range(NT):
                for q in range(4):
                    last = nc.tensor.transpose(pc[:rows(t), (t * 4 + q) * H:(t * 4 + q + 1) * H],
                                               row[:, q, t * P:t * P + rows(t)], ident[:H, :H])
            last.then_inc(cols_ps, 1)
            nc.tensor.matmul(pd[:, 0:H * 2 * NC], ones4[:, :], decmd[:, :, :].rearrange("p h c -> p (h c)"),
                             start=True, stop=True).then_inc(dec_ps, 1)

        @block.scalar
        def _(act):
            act.wait_ge(z_done, 1)
            nc.scalar.activation(ez[:, :], ez[:, :], ACT.Exp, scale=-1.0).then_inc(e1_done, 1)
            act.wait_ge(e1_done, 1)
            nc.scalar.activation(ez[:, :], ez[:, :], ACT.Ln, bias=1.0).then_inc(e2_done, 1)
            act.wait_ge(cols_out, 1)
            nc.scalar.activation(cols[:, :, 1:4, :], cols[:, :, 1:4, :], ACT.Exp).then_inc(exp_out, 1)
            act.wait_ge(dec_ps, 1)
            nc.scalar.activation(dec[:, :, :], pd[:, 0:H * 2 * NC].rearrange("p (h c) -> p h c", h=H),
                                 ACT.Exp).then_inc(exp_out, 1)

        @block.vector
        def _(dve):
            v = nc.vector
            ch = Chain(dve, chain)
            dve.wait_ge(gate_in, 96)
            ch.mark(v.memset(shift[:, :], 0.0))
            ch.mark(v.memset(mprev[:, :], 0.0))
            ch.mark(v.memset(cols[:, :, :, :], 0.0))
            dve.wait_ge(pre_done, 1)
            for c in range(3):
                s = slice(c * TC, (c + 1) * TC)
                ch.mark(v.tensor_scalar(ig[:, s], pi[c][:H, 0:TC], bif[:, 0:1], None, ALU.add))
                ch.link(v.tensor_scalar(zf[:, s], pf[c][:H, 0:TC], bif[:, 1:2], None, ALU.add))
            v.scalar_tensor_tensor(ez[:, :], zf[:, :], -1.0, zf[:, :], ALU.mult, ALU.max).then_inc(z_done, 1)
            dve.wait_ge(e2_done, 1)
            ch.link(v.scalar_tensor_tensor(lf[:, :], zf[:, :], 0.0, ez[:, :], ALU.min, ALU.subtract))
            ch.link(v.tensor_tensor_scan(b[:, :], msk[:, :], lf[:, :], 0.0, ALU.mult, ALU.add))
            ch.mark(v.tensor_tensor(row[:, 0, :], ig[:, :], b[:, :], ALU.subtract))
            bl = b[:, 0:SEQ].rearrange("p (c t) -> p c t", t=P)[:, :, P - 1]
            ch.link(v.tensor_copy(shift[:, P:SEQ].rearrange("p (c t) -> p c t", t=P)[:, :, 0], bl[:, 0:NC - 1]))
            ch.mark(v.tensor_tensor_scan(M[:, 0:SEQ], shift[:, :], row[:, 0, 0:SEQ], 0.0, ALU.add, ALU.max))
            ch.link(v.tensor_tensor(M[:, SEQ:T], m_in[:, :], row[:, 0, SEQ:T], ALU.max))
            M3 = M[:, 0:SEQ].rearrange("p (c t) -> p c t", t=P)
            ml = M3[:, :, P - 1]
            ch.mark(v.tensor_tensor(mnew[:, NC:NC + NS], M[:, SEQ:T], b[:, SEQ:T], ALU.add))
            ch.link(v.tensor_tensor(mnew[:, 0:NC], ml, bl, ALU.add))
            ch.link(v.tensor_copy(mprev[:, 1:NC], mnew[:, 0:NC - 1]))

            def c3(ap):
                return ap[:, 0:SEQ].rearrange("p (c t) -> p c t", t=P)
            ch.mark(v.tensor_tensor(c3(row[:, 1, :]), mprev[:, :].unsqueeze(2).broadcast_to([H, NC, P]), M3,
                                    ALU.subtract))
            ch.mark(v.tensor_tensor(row[:, 1, SEQ:T], m_in[:, :], M[:, SEQ:T], ALU.subtract))
            ch.mark(v.scalar_tensor_tensor(row[:, 2, :], M[:, :], -1.0, b[:, :], ALU.mult, ALU.subtract))
            ch.mark(v.tensor_tensor(c3(row[:, 3, :]), c3(row[:, 0, :]), ml.unsqueeze(2).broadcast_to([H, NC, P]),
                                    ALU.subtract))
            ch.link(v.tensor_tensor(row[:, 3, SEQ:T], row[:, 0, SEQ:T], M[:, SEQ:T], ALU.subtract))
            for h in range(H):
                ch.mark(v.tensor_scalar(negmd[:, h, :], M[:, 0:SEQ], delta[:, h:h + 1], -1.0, ALU.mult, ALU.mult))
                ch.mark(v.tensor_scalar(decmd[:, h, 0:NC], c3(row[:, 1, :])[:, :, P - 1], delta[:, h:h + 1], None,
                                        ALU.mult))
                last = v.tensor_scalar(decmd[:, h, NC:2 * NC], row[:, 1, SEQ:T], delta[:, h:h + 1], None, ALU.mult)
            last.then_inc(rows_done, 1)
            dve.wait_ge(cols_ps, 1)
            pc4 = pc[:, 0:NT * 16].rearrange("p (t q h) -> p t q h", q=4, h=H)
            ch.link(v.tensor_copy(cols[:, 0:NC, :, :], pc4[:, 0:NC]))
            v.tensor_copy(cols[:NS, NC, :, :], pc4[:NS, NC]).then_inc(cols_out, 1)

    head_loop(nc, A, O, sb, ps, sem, ident, xnT, mix, cols, dec, negmd, w, w_in, False)
    clear("h_")
    head_loop(nc, A, O, sb, ps, sem, ident, xnT, mix, cols, dec, negmd, w, w_in, True)
    heads.close()

    with ExitStack() as st, nc.Block() as block:
        mixT = sb(st, "mixT", [P, ND, T])
        wo = sb(st, "wo", [P, ND, D])
        x2 = sb(st, "x2", [P, NT, D])
        junk = sb(st, "sq_junk2", [P, D])
        ss = sb(st, "ss2", [P, NT])
        rstd = sb(st, "rstd2", [P, NT])
        bank = [ps(st, f"o_tr{i}") for i in range(4)]
        py = [ps(st, f"o_y{i}") for i in range(4)]
        x_in = sem("x2_in")
        wo_in, ones_set, mt_done, mt_free, y_done, x2_done, sq_done, ms_done, root_done, rstd_done, hn_done, h_done, h_free = (
            sem(n) for n in ("wo_in", "o_ones", "o_mt_done", "o_mt_free", "o_y_done", "o_x2", "o_sq", "o_ms",
                             "o_root", "o_rstd", "o_hn", "o_h_done", "o_h_free"))

        @block.sync
        def _(sp):
            sp.dma_start(wo[:, :, :], A["w_out"]).then_inc(wo_in, 16)
            for t in range(NT):
                sp.dma_start(x2[:rows(t), t, :], A["x"][t * P:t * P + rows(t), :]).then_inc(x_in, 16)
            for t in range(NT):
                sp.wait_ge(x2_done, 2 * t + 2)
                sp.dma_start(x2_dram[t * P:t * P + rows(t), :], x2[:rows(t), t, :]).then_inc(x2_saved, 16)
            sp.wait_ge(x2_saved, 16 * NT)

        @block.tensor
        def _(pe):
            transpose_units_pe(nc, pe, mix, ident, bank, mt_done, mt_free, lambda g: None)
            pe.wait_ge(wo_in, 16)
            pe.wait_ge(mt_free, len(UNITS))
            for t in range(NT):
                for n in range(2):
                    u = 2 * t + n
                    if u >= 4:
                        pe.wait_ge(x2_done, u - 3)
                    for k in range(ND):
                        last = nc.tensor.matmul(py[u % 4][:rows(t), :], mixT[:, k, t * P:t * P + rows(t)],
                                                wo[:, k, n * 512:(n + 1) * 512], start=(k == 0), stop=(k == ND - 1))
                    last.then_inc(y_done, 1)
            transpose_units_pe(nc, pe, mix, ident, bank, h_done, h_free, lambda g: pe.wait_ge(hn_done, (4, 8, NT)[g]))

        @block.scalar
        def _(act):
            act.wait_ge(ones_set, 1)
            for t in range(NT):
                act.wait_ge(x2_done, 2 * t + 2)
                if t:
                    act.wait_ge(sq_done, t)
                nc.scalar.activation(junk[:rows(t), :], x2[:rows(t), t, :], ACT.Square,
                                     accum_out=ss[:rows(t), t:t + 1]).then_inc(sq_done, 1)
            act.wait_ge(ms_done, 1)
            nc.scalar.activation(rstd[:, :], ss[:, :], ACT.Sqrt).then_inc(root_done, 1)
            act.wait_ge(rstd_done, 1)
            for t in range(NT):
                nc.scalar.activation(mix[:rows(t), t, :], x2[:rows(t), t, :], ACT.Copy,
                                     scale=rstd[:rows(t), t:t + 1]).then_inc(hn_done, 1)

        @block.vector
        def _(dve):
            nc.vector.memset(ss[:, :], 1.0).then_inc(ones_set, 1)
            transpose_units_out(nc, dve, mixT, gnm, bank, mt_done, mt_free)
            dve.wait_ge(x_in, 16 * NT)
            for t in range(NT):
                for n in range(2):
                    u = 2 * t + n
                    s = slice(n * 512, (n + 1) * 512)
                    dve.wait_ge(y_done, u + 1)
                    nc.vector.tensor_tensor(x2[:rows(t), t, s], py[u % 4][:rows(t), :], x2[:rows(t), t, s],
                                            ALU.add).then_inc(x2_done, 1)
            dve.wait_ge(sq_done, NT)
            nc.vector.tensor_scalar(ss[:, :], ss[:, :], 1.0 / D, EPS, ALU.mult, ALU.add).then_inc(ms_done, 1)
            dve.wait_ge(root_done, 1)
            nc.vector.reciprocal(rstd[:, :], rstd[:, :]).then_inc(rstd_done, 1)
            transpose_units_out(nc, dve, hnT, gffn, bank, h_done, h_free)


def head_loop(nc, A, O, sb, ps, sem, ident, xnT, mix, cols, dec, negmd, w, w_in, ret):
    n0 = "r" if ret else "m"
    base = H if ret else 0
    W = P if ret else P + 1
    with ExitStack() as st, nc.Block() as block:
        pr = sb(st, n0 + "_pr", [P, NT, PROJ])
        gate = sb(st, n0 + "_gate", [P, 2, NT, P])
        dm = sb(st, n0 + "_dm", [P, H if ret else 1, SEQ if not ret else P])
        hh = sb(st, n0 + "_h", [P, NT, P])
        hx = sb(st, n0 + "_hx", [P, P + 1])
        den = sb(st, n0 + "_den", [P, 2])
        stats = sb(st, n0 + "_stats", [P, NT, 6])
        mv = sb(st, n0 + "_mv", [P, NT, 2])
        qkT = sb(st, n0 + "_qkT", [P, 2, 2 * P])
        sd = sb(st, n0 + "_sd", [P, P])
        ka = sb(st, n0 + "_ka", [P, P])
        C = sb(st, n0 + "_C", [P, H, W])
        cs = sb(st, n0 + "_cs", [P, H, NS, W])
        kbig = sb(st, n0 + "_kbig", [NS, NS, P])
        qm = sb(st, n0 + "_qm", [P, NS, P])
        dmask = sb(st, n0 + "_dmask", [NS, NS, P])
        if ret:
            rot = sb(st, "r_rot", [P, NT, 2, 2, P // 2])
            cosin = sb(st, "r_cosin", [P, 2, NT, P // 2])
            m1 = sb(st, "r_m1", [P, 2, 2, P // 2])
            m2 = sb(st, "r_m2", [P, 2, 2, P // 2])
            rcol = sb(st, "r_col", [P, 3, H])
            rdec1 = sb(st, "r_dec1", [P, H])
            pos = sb(st, "r_pos", [NS, 1], I32)
            posf = sb(st, "r_posf", [NS, 1])
            inv = sb(st, "r_inv", [NS, P // 2])
            ang = sb(st, "r_ang", [NS, 2, P // 2])
            turns = sb(st, "r_turns", [NS, 2, P // 2])
        else:
            neg = sb(st, "m_neg", [P, P])
            ones4 = sb(st, "m_ones4", [H, P])
            pb = ps(st, "m_pb", (P, 1024))
        pp = [ps(st, f"{n0}_pp{i}") for i in range(2)]
        pt, pS, pA, pU = (ps(st, f"{n0}_p{i}") for i in "tSAU")
        names = ("const_in preset bc_done arg_done dm_done pj_done pj_out tr_done "
                 "tr_out rot_done s_done sd_done ka_done a_done h_done u_done c_done kb_done "
                 "up_done cs_done hs_done heads_done root_done out_c out_cs chain cs_in var_done").split()
        S = {n: sem("h_" + n) for n in names}
        TOK = [0, 1, 2, 3, NC, 4, 5, 6, 7]

        @block.sync
        def _(sp):
            loads = [(dmask[:, :, :], A["dmask"])]
            if ret:
                loads += [(dm[:, :, :], A["dmat"]), (cosin[:, :, 0:NC, :], A["cosin"]), (rcol[:, :, :], A["rcol"]),
                          (rdec1[:, :], A["rdec1"]), (pos[:, :], A["pos"]), (inv[:, :], A["inv"])]
            else:
                loads += [(neg[:, :], A["neg"]), (ones4[:, :], A["ones4"])]
            for dst, src in loads:
                sp.dma_start(dst, src).then_inc(S["const_in"], 16)
            sp.dma_start(cs[:, :, :, :], A["cs" + n0]).then_inc(S["cs_in"], 16)
            for h in range(H):
                if base + h + 2 < 2 * H:
                    sp.wait_ge(S["pj_done"], NT * (h + 1))
                    sp.dma_start(w[:, h % 2, :, :], A["w_heads"][base + h + 2]).then_inc(w_in[h % 2], 16)
                sp.wait_ge(S["cs_done"], NS * (h + 1))
                sp.dma_start(O["cs" + n0][h], cs[:, h, :, :]).then_inc(S["out_cs"], 16)
                sp.wait_ge(S["c_done"], NC * (h + 1) + 1)
                sp.dma_start(O["c" + n0][h], C[:, h, :]).then_inc(S["out_c"], 16)
            sp.wait_ge(S["out_c"], 16 * H)
            sp.wait_ge(S["out_cs"], 16 * H)

        @block.tensor
        def _(pe):
            mm, tp = nc.tensor.matmul, nc.tensor.transpose
            pe.sem_inc(S["hs_done"], 1)
            pe.sem_inc(S["a_done"], 1)
            pe.wait_ge(S["const_in"], 16 * (7 if ret else 3))
            with pe.Fori(0, H) as h:
                hb = h % 2

                def project(i, blocks):
                    if i >= NT:
                        return
                    t = TOK[i]
                    if 0 in blocks:
                        if i == 0:
                            pe.wait_ge(w_in[0], ((h + 2) // 2) * 16 + 8 * base)
                            pe.wait_ge(w_in[1], ((h + 3) // 2) * 16 + 8 * base)
                    for k in blocks:
                        last = mm(pp[i % 2][:rows(t), :], xnT[:, k, t * P:t * P + rows(t)], w[:, hb, k, :],
                                  start=(k == 0), stop=(k == ND - 1))
                    if ND - 1 in blocks:
                        last.then_inc(S["pj_done"], 1)

                def turn(i):
                    if i >= NT:
                        return
                    t = TOK[i]
                    if ret:
                        pe.wait_ge(S["rot_done"], 2 * (h * NT + i + 1))
                    else:
                        pe.wait_ge(S["pj_out"], h * NT + i + 1)
                    for q in range(2 if t < NC else 1):
                        src = rot[:, t, q, :, :].rearrange("p a b -> p (a b)") if ret else pr[:, t, q * P:(q + 1) * P]
                        last = tp(pt[:, q * P:(q + 1) * P], src, ident[:, :])
                    last.then_inc(S["tr_done"], 1)

                if not ret:
                    for i in range(2):
                        last = mm(pb[:, i * 512:(i + 1) * 512], ones4[:, :], negmd[:, h, i * 512:(i + 1) * 512],
                                  start=True, stop=True)
                    last.then_inc(S["bc_done"], 1)
                for i in range(2):
                    project(i, range(ND))
                turn(0)
                for i, t in enumerate(TOK):
                    project(i + 2, range(4))
                    pe.wait_ge(S["tr_out"], h * NT + i + 1)
                    if t < NC:
                        mm(pS[:, 0:P], qkT[:, t % 2, P:2 * P], qkT[:, t % 2, 0:P], start=True,
                           stop=True).then_inc(S["s_done"], 1)
                        pe.wait_ge(S["ka_done"], h * NC + t + 1)
                        pe.wait_ge(S["c_done"], h * NC + t + 1)
                        mm(pU[:, 0:W], ka[:, :], pr[:, t, V0:V0 + W], start=True, stop=True).then_inc(S["u_done"], 1)
                        project(i + 2, range(4, ND))
                        turn(i + 1)
                        pe.wait_ge(S["sd_done"], h * NC + t + 1)
                        pe.wait_ge(S["h_done"], h * NT + i + 1)
                        last = mm(pA[:, 0:W], sd[:, :], pr[:, t, V0:V0 + W], start=True, stop=True)
                        if t:
                            last = mm(pA[:, 256:256 + W], qkT[:, t % 2, 0:P], C[:, h, :], start=True, stop=True)
                        last.then_inc(S["a_done"], 1)
                    else:
                        pe.wait_ge(S["kb_done"], h + 1)
                        pe.wait_ge(S["c_done"], h * NC + TOK.index(NC) + 1)
                        pe.wait_ge(S["sd_done"], h * NC + TOK.index(NC))
                        for n in range(NS):
                            if n >= 2:
                                pe.wait_ge(S["cs_done"], h * NS + n - 1)
                            mm((pU, pS)[n % 2][:, 0:W], kbig[:, n, :], pr[:NS, NC, V0:V0 + W], start=True,
                               stop=True).then_inc(S["up_done"], 1)
                            if 1 <= n <= ND - 4:
                                project(i + 2, (3 + n,))
                        turn(i + 1)
                        pe.wait_ge(S["cs_done"], h * NS + NS)
                        pe.wait_ge(S["h_done"], h * NT + i + 1)
                        for n in range(NS):
                            last = mm(pA[:, 0:W], qm[:, n, :], cs[:, h, n, :], start=(n == 0), stop=(n == NS - 1))
                        last.then_inc(S["hs_done"], 1)

        @block.scalar
        def _(act):
            ac = nc.scalar.activation
            act.wait_ge(S["preset"], 1)
            if ret:
                act.wait_ge(S["preset"], 2)
                ac(cosin[:NS, 1, NC, :], ang[:, 1, :], ACT.Sin)
                ac(cosin[:NS, 0, NC, :], ang[:, 0, :], ACT.Sin).then_inc(S["preset"], 1)
            with act.Fori(0, H) as h:
                act.wait_ge(S["heads_done"], h + 1)
                act.wait_ge(S["hs_done"], h + 1)
                for i, t in enumerate(TOK):
                    r = rows(t)
                    act.wait_ge(S["pj_done"], h * NT + i + 1)
                    ac(gate[:r, h % 2, t, :], pp[i % 2][:r, 3 * P:4 * P], ACT.Silu if ret else ACT.Sigmoid)
                    ac(pr[:r, t, 0:3 * P], pp[i % 2][:r, 0:3 * P], ACT.Copy).then_inc(S["pj_out"], 1)
                    if t == 0 and not ret:
                        act.wait_ge(S["arg_done"], h * NC + NC)
                        ac(dm[:, 0, :], dm[:, 0, :], ACT.Exp).then_inc(S["dm_done"], 1)
                    act.wait_ge(S["tr_done"], h * NT + i + 1)
                    if t == 0:
                        act.wait_ge(S["a_done"], h * NC + 1)
                    elif t >= 2:
                        act.wait_ge(S["a_done"], h * NC + (t if t < NC else 1))
                    if t < NC:
                        ac(qkT[:, t % 2, :], pt[:, 0:2 * P], ACT.Copy).then_inc(S["tr_out"], 1)
                    else:
                        ac(qm[:, :, :].rearrange("p a b -> p (a b)")[:, 0:NS * P:P + 1], pt[:, 0:NS],
                           ACT.Copy).then_inc(S["tr_out"], 1)
                act.wait_ge(S["var_done"], h + 1)
                ac(mv[:, :, 1], mv[:, :, 1], ACT.Sqrt).then_inc(S["root_done"], 1)

        @block.vector
        def _(dve):
            v = nc.vector
            ch = Chain(dve, S["chain"])
            ch.mark(v.memset(qm[:, :, :], 0.0))
            ch.mark(v.memset(stats[:, :, :], 1.0))
            if ret:
                ch.mark(v.memset(rot[:, NC], 1.0))
            ch.mark(v.memset(hh[:, :, :], 0.0))
            ch.mark(v.memset(gate[:, :, :, :], 1.0))
            dve.sem_inc(S["c_done"], 1)
            dve.sem_inc(S["h_done"], 1)
            dve.sem_inc(S["heads_done"], 2)
            v.memset(pr[:, :, :], 1.0).then_inc(S["preset"], 1)
            dve.wait_ge(S["const_in"], 16 * (7 if ret else 3))
            if ret:
                TP = [6.28125, 253 / 131072, 2 * np.pi - 6.28125 - 253 / 131072]
                ch.link(v.tensor_copy(posf[:, :], pos[:, :]))
                ch.link(v.tensor_scalar(ang[:, 1, :], inv[:, :], posf[:, 0:1], None, ALU.mult))
                ch.link(v.tensor_scalar(turns[:, 1, :], ang[:, 1, :], float(1 / (2 * np.pi)), 0.0, ALU.mult, ALU.add))
                ch.link(v.tensor_scalar(turns[:, 0, :], turns[:, 1, :], 0.25, 12582912.0, ALU.add, ALU.add))
                ch.link(v.tensor_scalar(turns[:, 1, :], turns[:, 1, :], 12582912.0, -12582912.0, ALU.add, ALU.add))
                ch.link(v.tensor_scalar(turns[:, 0, :], turns[:, 0, :], -12582912.0, 0.0, ALU.add, ALU.add))
                ch.link(v.tensor_copy(ang[:, 0, :], ang[:, 1, :]))
                for c in TP:
                    ch.link(v.scalar_tensor_tensor(ang[:, :, :], turns[:, :, :], -float(np.float32(c)), ang[:, :, :],
                                                   ALU.mult, ALU.add))
                ch.link(v.tensor_scalar(ang[:, 0, :], ang[:, 0, :], float(np.pi / 2), 0.0, ALU.add, ALU.add))
                v.tensor_scalar(ang[:, :, :], ang[:, :, :], 3.1415925, -3.1415925, ALU.min,
                                ALU.max).then_inc(S["preset"], 1)
                dve.wait_ge(S["preset"], 3)
            with dve.Fori(0, H) as h:
                ch.enter(h, PER["ret" if ret else "mlstm"])
                g0 = h + base
                if not ret:
                    dve.wait_ge(S["bc_done"], h + 1)
                    for c in range(NC):
                        v.scalar_tensor_tensor(dm[:, 0, c * P:(c + 1) * P], pb[:, c * P:(c + 1) * P],
                                               cols[:, c, 0, bass.ds(h, 1)], neg[:, :], ALU.add,
                                               ALU.min).then_inc(S["arg_done"], 1)

                def rotate(i):
                    t = TOK[i]
                    r = rows(t)
                    dve.wait_ge(S["pj_out"], h * NT + i + 1)
                    cos = cosin[:r, 0, t, :].unsqueeze(1).broadcast_to([r, 4, P // 2])
                    sin = cosin[:r, 1, t, :].unsqueeze(1).broadcast_to([r, 4, P // 2])
                    qk4 = pr[:r, t, 0:2 * P].rearrange("p (i b) -> p i b", i=4)
                    ch.mark(v.tensor_tensor(m1[:r].rearrange("p i a b -> p (i a) b"), qk4, cos, ALU.mult))
                    ch.link(v.tensor_tensor(m2[:r].rearrange("p i a b -> p (i a) b"), qk4, sin, ALU.mult))
                    v.tensor_tensor(rot[:r, t, :, 0, :], m1[:r, :, 0, :], m2[:r, :, 1, :],
                                    ALU.subtract).then_inc(S["rot_done"], 1)
                    v.tensor_tensor(rot[:r, t, :, 1, :], m2[:r, :, 0, :], m1[:r, :, 1, :],
                                    ALU.add).then_inc(S["rot_done"], 1)

                if ret:
                    rotate(0)
                for i, t in enumerate(TOK):
                    r = rows(t)
                    if ret:
                        winter, acol, dcol = rcol[:, 0, bass.ds(h, 1)], rcol[:, 1, bass.ds(h, 1)], rcol[:, 2, bass.ds(h, 1)]
                        kk = rot[:r, t, 1, :, :].rearrange("p a b -> p (a b)")
                        dve.wait_ge(S["rot_done"], 2 * (h * NT + i + 1))
                    else:
                        winter, acol = cols[:r, t, 1, bass.ds(h, 1)], cols[:r, t, 3, bass.ds(h, 1)]
                        dcol = dec[:, h, t:t + 1] if t < NC else None
                        kk = pr[:r, t, K0:K0 + P]
                        dve.wait_ge(S["pj_out"], h * NT + i + 1)
                    if t < NC:
                        v.tensor_scalar(ka[:, :], kk, acol, SCALE, ALU.mult, ALU.mult).then_inc(S["ka_done"], 1)
                        dve.wait_ge(S["s_done"], h * NC + t + 1)
                        if not ret and t == 0:
                            dve.wait_ge(S["dm_done"], h + 1)
                        dmt = dm[:, h, :] if ret else dm[:, 0, t * P:(t + 1) * P]
                        v.scalar_tensor_tensor(sd[:, :], pS[:, 0:P], SCALE, dmt, ALU.mult,
                                               ALU.mult).then_inc(S["sd_done"], 1)
                        if ret and i + 1 < NT:
                            rotate(i + 1)
                        dve.wait_ge(S["a_done"], h * NC + t + 2)
                        dve.wait_ge(S["u_done"], h * NC + t + 1)
                        if t == 0:
                            v.tensor_copy(C[:, h, :], pU[:, 0:W]).then_inc(S["c_done"], 1)
                            ch.link(v.tensor_copy(hx[:, 0:W], pA[:, 0:W]))
                        else:
                            dve.wait_ge(S["c_done"], h * NC + t + 1)
                            v.scalar_tensor_tensor(C[:, h, :], C[:, h, :], dcol, pU[:, 0:W], ALU.mult,
                                                   ALU.add).then_inc(S["c_done"], 1)
                            ch.link(v.tensor_copy(hx[:, 0:W], pA[:, 0:W]))
                            ch.link(v.scalar_tensor_tensor(hx[:, 0:W], pA[:, 256:256 + W], winter, hx[:, 0:W],
                                                           ALU.mult, ALU.add))
                    else:
                        v.scalar_tensor_tensor(kbig[:, :, :], kk.unsqueeze(1).broadcast_to([NS, NS, P]),
                                               1.0 if ret else acol, dmask[:, :, :], ALU.mult,
                                               ALU.mult).then_inc(S["kb_done"], 1)
                        dve.wait_ge(S["cs_in"], 16)
                        for n in range(NS):
                            dn = rdec1[:, bass.ds(h, 1)] if ret else dec[:, h, NC + n:NC + n + 1]
                            dve.wait_ge(S["up_done"], h * NS + n + 1)
                            v.scalar_tensor_tensor(cs[:, h, n, :], cs[:, h, n, :], dn, (pU, pS)[n % 2][:, 0:W], ALU.mult,
                                                   ALU.add).then_inc(S["cs_done"], 1)
                        if ret:
                            rotate(i + 1)
                        dve.wait_ge(S["hs_done"], h + 2)
                        ch.link(v.tensor_copy(hx[:r, 0:W], pA[:r, 0:W]))
                    if not ret:
                        ch.link(v.tensor_scalar(den[:r, 0:1], hx[:r, P:P + 1], -1.0, cols[:r, t, 2, bass.ds(h, 1)],
                                                ALU.mult, ALU.max))
                        ch.link(v.tensor_tensor(den[:r, 0:1], den[:r, 0:1], hx[:r, P:P + 1], ALU.max))
                        ch.link(v.reciprocal(den[:r, 1:2], den[:r, 0:1]))
                        ch.link(v.tensor_scalar(hh[:r, t, :], hx[:r, 0:P], den[:r, 1:2], None, ALU.mult))
                    else:
                        ch.link(v.tensor_copy(hh[:r, t, :], hx[:r, 0:P]))
                    v.bn_stats(stats[:r, t, :], hh[:r, t, :]).then_inc(S["h_done"], 1)
                dve.wait_ge(S["h_done"], h * NT + NT + 1)
                ch.wait(ch.n)
                ch.mark(v.memset(den[:, 0:1], 1.0))
                for t in TOK:
                    ch.mark(v.bn_aggr(mv[:, t, :], stats[:, t, :]))
                ch.wait(ch.n)
                v.tensor_scalar(mv[:, :, 1], mv[:, :, 1], EPS, None, ALU.add).then_inc(S["var_done"], 1)
                dve.wait_ge(S["root_done"], h + 1)
                ch.link(v.reciprocal(mv[:, :, 1], mv[:, :, 1]))
                for t in TOK:
                    ch.mark(v.tensor_scalar(hh[:, t, :], hh[:, t, :], mv[:, t, 0:1], mv[:, t, 1:2], ALU.subtract,
                                            ALU.mult))
                ch.wait(ch.n)
                v.tensor_tensor(mix[:, :, bass.ds(g0 * P, P)], hh[:, :, :], gate[:, h % 2, :, :],
                                ALU.mult).then_inc(S["heads_done"], 1)
                dve.wait_ge(S["heads_done"], h + 3)
                ch.leave(H)


PER = {"mlstm": 72, "ret": 63, "select": 315, "decode": 16}


def routing_stages(nc, A, own, sb, ps, sem, ident, hnT, g_dram, g_tail, load_rows):
    e1T = sb(own, "e1T", [P, T])
    STEP = 8
    e2gT = sb(own, "e2gT", [P, 2, T + STEP])
    iota = sb(own, "iota", [P, NK])
    iota_in = sem("iota_in")
    with ExitStack() as both:
        idx = sb(both, "idx", [P, 4, NT, 2, 2, TOPK])
        tops = sb(both, "tops", [P, 4, NT, 2, TOPK])
        posn = sb(both, "posn", [P, 4, NT, 2, TOPK], U32)

        with ExitStack() as st, nc.Block() as block:
            wq = sb(st, "wq", [P, 2, ND, 2 * P])
            sk = sb(st, "sk", [P, PH, 2, NK])
            qT = sb(st, "qT", [P, 2, 2, T])
            tv = sb(st, "tv", [P, 4, 2, TOPK])
            ti = sb(st, "ti", [P, NT, 2, 2, TOPK], U32)
            rest = sb(st, "rest", [P, 4, 2, NK])
            cand = sb(st, "cand", [P, 4, TOPK * TOPK])
            crest = sb(st, "crest", [P, 4, TOPK * TOPK])
            ts_ = sb(st, "ts", [P, NT, 2, TOPK])
            tp_ = sb(st, "tp", [P, NT, 2, TOPK], U32)
            spare, carrier, zero1 = (sb(st, "spare" + x, [P, 1]) for x in "abc")
            pq = [ps(st, f"s_q{i}") for i in range(3)]
            pscore = [ps(st, f"s_s{i}", (P, 4, 2, NK)) for i in range(2)]
            wq_in = [sem(f"wq_in{i}") for i in range(2)]
            sk_in, q_done, q_out, score_done, score_used, chain = (
                sem(n) for n in ("sk_in", "q_done", "q_out", "score_done", "score_used", "s_chain"))
            TC = T // 3

            @block.sync
            def _(sp):
                sp.dma_start(iota[:, :], A["iota"]).then_inc(iota_in, 16)
                sp.dma_start(sk[:, :, :, :], A["sub_keys"]).then_inc(sk_in, 16)
                for s in range(2):
                    sp.dma_start(wq[:, s, :, :], A["w_query"][s]).then_inc(wq_in[s], 16)
                for pr in range(3):
                    for s in range(2):
                        sp.wait_ge(q_done, 12 * pr + 6 * s + 6)
                        sp.dma_start(wq[:, s, :, :], A["w_query"][2 * pr + 2 + s]).then_inc(wq_in[s], 16)

            @block.tensor
            def _(pe):
                pe.sem_inc(score_done, 1)
                pe.wait_ge(sk_in, 16)
                with pe.Fori(0, 4) as pr:
                    for s in range(2):
                        pe.wait_ge(wq_in[s], 16 * pr + 16)
                        for gi, g in enumerate(GROUPS):
                            for c, side in [(c, side) for c in ((0, 1), (2,), ())[gi] for side in range(2)]:
                                n = 6 * s + 2 * c + side
                                if n >= 3:
                                    pe.wait_ge(q_out, 12 * pr + n - 2)
                                for k in range(ND):
                                    last = nc.tensor.matmul(pq[n % 3][:, 0:TC], wq[:, s, k, side * P:(side + 1) * P],
                                                            hnT[:, k, c * TC:(c + 1) * TC], start=(k == 0),
                                                            stop=(k == ND - 1))
                                last.then_inc(q_done, 1)
                            if gi < 2:
                                pe.wait_ge(q_out, 12 * pr + 6 * s + (4, 6)[gi])
                            u = 3 * s + gi
                            if gi < 2:
                                pe.wait_ge(score_used, pr * 6 + u + 1)
                            for q, t in enumerate(g):
                                for side in range(2):
                                    if gi == 1 and q == len(g) - 1 and side == 1:
                                        pe.wait_ge(score_used, pr * 6 + u + 2)
                                    last = nc.tensor.matmul(pscore[u % 2][:rows(t), q, side, :],
                                                            qT[:, s, side, t * P:t * P + rows(t)],
                                                            sk[:, 2 * pr + s, side, :], start=True, stop=True)
                            last.then_inc(score_done, 1)

            @block.scalar
            def _(act):
                with act.Fori(0, 4) as pr:
                    for s in range(2):
                        for c in range(3):
                            for side in range(2):
                                n = 6 * s + 2 * c + side
                                act.wait_ge(q_done, 12 * pr + n + 1)
                                if side == 0 and c == 0:
                                    act.wait_ge(score_done, pr * 6 + 1)
                                nc.scalar.activation(qT[:, s, side, c * TC:(c + 1) * TC], pq[n % 3][:, 0:TC],
                                                     ACT.Copy).then_inc(q_out, 1)

            @block.vector
            def _(dve):
                v = nc.vector
                ch = Chain(dve, chain)

                def tick():
                    ch.wait(ch.n)
                    ch.mark(v.tensor_copy(spare[:, :], zero1[:, :]))

                dve.sem_inc(score_used, 2)
                ch.link(v.memset(zero1[:, :], 0.0))
                ch.mark(v.memset(idx[:, :, :, :, :, :].rearrange("p a b c d e -> p (a b c d e)"), 0.0))
                ch.mark(v.memset(ti[:, :, :, :, :].rearrange("p a b c d -> p (a b c d)"), 0))
                ch.mark(v.memset(ts_[:, :, :, :].rearrange("p a b c -> p (a b c)"), 0.0))
                ch.link(v.memset(tp_[:, :, :, :].rearrange("p a b c -> p (a b c)"), 0))
                with dve.Fori(0, 4) as pr:
                    ch.enter(pr, PER["select"])
                    for s in range(2):
                        for gi, g in enumerate(GROUPS):
                            u, r, t0, G = 3 * s + gi, rows(g[0]), g[0], len(g)
                            both_sides = [(q, side) for q in range(G) for side in range(2)]
                            sc = pscore[u % 2]
                            dve.wait_ge(score_done, pr * 6 + u + 2)
                            ch.mark(v.tensor_copy(carrier[:, :], zero1[:, :]))
                            for q, side in both_sides:
                                ch.mark(v.max(tv[:r, q, side, 0:8], sc[:r, q, side, :]))
                            tick()
                            for q, side in both_sides:
                                ch.mark(v.max_index(ti[:r, t0 + q, s, side, 0:8], tv[:r, q, side, 0:8],
                                                    sc[:r, q, side, :]))
                                last = v.match_replace(rest[:r, q, side, :], tv[:r, q, side, 0:8],
                                                       sc[:r, q, side, :], LOW)
                                if (q, side) != both_sides[-1]:
                                    ch.mark(last)
                            last.then_inc(score_used, 1)
                            dve.wait_ge(score_used, pr * 6 + u + 3)
                            tick()
                            for q, side in both_sides:
                                ch.mark(v.max(tv[:r, q, side, 8:16], rest[:r, q, side, :]))
                            ch.wait(ch.n)
                            ch.mark(v.tensor_tensor(
                                cand[:r, 0:G, :].rearrange("p q (a b) -> p q a b", b=TOPK),
                                tv[:r, 0:G, 0, :].unsqueeze(3).broadcast_to([r, G, TOPK, TOPK]),
                                tv[:r, 0:G, 1, :].unsqueeze(2).broadcast_to([r, G, TOPK, TOPK]), ALU.add))
                            for q, side in both_sides:
                                ch.mark(v.max_index(ti[:r, t0 + q, s, side, 8:16], tv[:r, q, side, 8:16],
                                                    rest[:r, q, side, :]))
                            tick()
                            for q in range(G):
                                ch.mark(v.max(ts_[:r, t0 + q, s, 0:8], cand[:r, q, :]))
                            tick()
                            for q in range(G):
                                ch.mark(v.match_replace(crest[:r, q, :], ts_[:r, t0 + q, s, 0:8], cand[:r, q, :], LOW))
                                ch.mark(v.max_index(tp_[:r, t0 + q, s, 0:8], ts_[:r, t0 + q, s, 0:8], cand[:r, q, :]))
                            tick()
                            for q in range(G):
                                ch.mark(v.max(ts_[:r, t0 + q, s, 8:16], crest[:r, q, :]))
                            tick()
                            for q in range(G):
                                ch.mark(v.max_index(tp_[:r, t0 + q, s, 8:16], ts_[:r, t0 + q, s, 8:16], crest[:r, q, :]))
                    ch.wait(ch.n)
                    F = NT * 2 * TOPK
                    ch.mark(v.tensor_copy(idx[:, pr].rearrange("p t s i k -> p (t s i k)"),
                                          ti[:, :, :, :, :].rearrange("p t s i k -> p (t s i k)")))
                    ch.mark(v.tensor_copy(tops[:, pr].rearrange("p t s k -> p (t s k)"),
                                          ts_[:, :, :, :].rearrange("p t s k -> p (t s k)")))
                    ch.link(v.tensor_copy(posn[:, pr].rearrange("p t s k -> p (t s k)"),
                                          tp_[:, :, :, :].rearrange("p t s k -> p (t s k)")))
                    ch.leave(4)

        with ExitStack() as st, nc.Block() as block:
            K8 = PH * TOPK
            i1 = sb(st, "d_i1", [P, 2, PH, TOPK])
            pu = sb(st, "d_pu", [P, K8], U32)
            ab_u = sb(st, "d_abu", [P, 2, K8], U32)
            ab = sb(st, "d_ab", [P, 2, K8])
            oh = sb(st, "d_oh", [P, 2, TOPK, 2, K8])
            se = sb(st, "d_se", [P, 2, PH, TOPK])
            sm = sb(st, "d_sum", [P, PH, 2])
            gt = sb(st, "d_gate", [P, 2, K8])
            pt = [ps(st, f"d_t{i}") for i in range(2)]
            diff_done, exp_done, oh_done, e_done, t_done, t_out, chain = (
                sem(n) for n in ("d_diff", "d_exp", "d_oh_done", "d_edone", "d_tdone", "d_tout", "d_chain"))

            def tiles(eng, body):
                with eng.Fori(0, NC // 2) as i:
                    body(2 * i, 0, P)
                    body(2 * i + 1, 1, P)
                body(NC, 0, NS)

            @block.tensor
            def _(pe):
                def body(t, b, r):
                    pe.wait_ge(t_out, t + 1)
                    pe.wait_ge(oh_done, t + 1)
                    for side in range(2):
                        for j in range(TOPK):
                            nc.tensor.matmul(pt[b][:, side * P:side * P + r], oh[:r, b, j, side, :], ident[:r, :r],
                                             start=(j == 0), stop=(j == TOPK - 1))
                    pe.wait_ge(e_done, t + 1)
                    nc.tensor.transpose(pt[b][:, 2 * P:2 * P + r], gt[:r, b, :], ident[:r, :r]).then_inc(t_done, 1)
                pe.sem_inc(t_done, 2)
                tiles(pe, body)

            @block.scalar
            def _(act):
                def body(t, b, r):
                    act.wait_ge(diff_done, t + 1)
                    nc.scalar.activation(se[:r, b], se[:r, b], ACT.Exp).then_inc(exp_done, 1)
                    act.wait_ge(t_done, t + 3)
                    for q, dst in enumerate((e1T, e2gT[:, 0, :], e2gT[:, 1, :])):
                        last = nc.scalar.activation(dst[:, bass.ds(t * P, r)], pt[b][:, q * P:q * P + r], ACT.Copy)
                    last.then_inc(t_out, 1)
                act.sem_inc(t_out, 2)
                tiles(act, body)

            @block.vector
            def _(dve):
                v = nc.vector
                ch = Chain(dve, chain)

                ch.mark(v.memset(e2gT[:, :, T:T + STEP], 0.0))

                def body(t, b, r):
                    for side in range(2):
                        ch.mark(v.tensor_copy(i1[:r, side, :, :].rearrange("p (a s) k -> p a s k", s=2),
                                              idx[:r, :, t, :, side, :]))
                    ch.mark(v.tensor_copy(pu[:r, :].rearrange("p (a x) -> p a x", a=4),
                                          posn[:r, :, t, :, :].rearrange("p a s k -> p a (s k)")))
                    dve.wait_ge(t_done, t + 1)
                    for a in range(4):
                        last = v.tensor_tensor(se[:r, b, 2 * a:2 * a + 2, :], tops[:r, a, t, :, :],
                                               tops[:r, a, t, :, 0:1].broadcast_to([r, 2, TOPK]), ALU.subtract)
                    last.then_inc(diff_done, 1)
                    ch.wait(ch.n)
                    ch.mark(v.tensor_scalar(ab_u[:r, 0, :], pu[:r, :], 4, None, ALU.logical_shift_right))
                    ch.link(v.tensor_scalar(ab_u[:r, 1, :], pu[:r, :], TOPK - 1, None, ALU.bitwise_and))
                    ch.link(v.tensor_copy(ab[:r, :, :], ab_u[:r, :, :]))
                    for j in range(TOPK):
                        last = v.scalar_tensor_tensor(
                            oh[:r, b, j, :, :].rearrange("p i (h k) -> p (i h) k", k=TOPK),
                            ab[:r, :, :].rearrange("p i (h k) -> p (i h) k", k=TOPK), float(j),
                            i1[:r, :, :, j:j + 1].rearrange("p i h o -> p (i h) o").broadcast_to([r, 2 * PH, TOPK]),
                            ALU.is_equal, ALU.mult)
                    last.then_inc(oh_done, 1)
                    dve.wait_ge(exp_done, t + 1)
                    ch.link(v.tensor_reduce(sm[:r, :, 0], se[:r, b], AX.X, ALU.add))
                    ch.link(v.reciprocal(sm[:r, :, 1], sm[:r, :, 0]))
                    v.tensor_tensor(gt[:r, b, :].rearrange("p (h k) -> p h k", k=TOPK), se[:r, b],
                                    sm[:r, :, 1:2].broadcast_to([r, PH, TOPK]), ALU.mult).then_inc(e_done, 1)
                    dve.wait_ge(e_done, t + 1)

                with dve.Fori(0, NC // 2) as i:
                    ch.enter(i, PER["decode"])
                    body(2 * i, 0, P)
                    body(2 * i + 1, 1, P)
                    ch.leave(NC // 2)
                body(NC, 0, NS)

    with ExitStack() as st, nc.Block() as block:
        HALF = STEP // 2
        OWN, SHARED = 2, 4
        one1 = sb(st, "one1", [P, 2, STEP, NK])
        one2 = sb(st, "one2", [P, 2, STEP, NK])
        few = sb(st, "few", [P, 2, 2, STEP - OWN])
        raw = sb(st, "raw", [P, 2, SHARED, NK])
        spare = sb(st, "g_spare", [P, 1])
        gbuf = sb(st, "gbuf", [P, 2, NK, SUB])
        pg = [ps(st, f"g_p{i}") for i in range(4)]
        raw_done, act_hot, few_in, carried, step_done, dve_hot, pool_hot, bank_full, bank_out = (
            sem(n) for n in ("g_raw", "g_act_hot", "g_few", "g_carried", "g_step", "g_dve_hot", "g_pool_hot", "g_full", "g_bank_out"))
        saved = [sem(f"g_saved{i}") for i in range(2)]

        def steps(eng, body):
            with eng.Fori(0, SEQ // STEP // 2) as i:
                body(2 * i, 0)
                body(2 * i + 1, 1)
            body(SEQ // STEP, 0)

        def gated(eng, b, k, e2, gate):
            return eng.tensor_scalar(one2[:, b, k, :], iota[:, :], e2, gate, ALU.is_equal, ALU.mult)

        @block.sync
        def _(sp):
            for s in range(2):
                sp.sem_inc(saved[s], 16)
            for s in range(2):
                load_rows(sp, s, s)
            with sp.Fori(0, NSUB // 2) as j:
                for s in range(2):
                    sp.wait_ge(bank_out, 32 * j + 16 * s + 20)
                    sp.dma_start(g_dram[2 * j + s], gbuf[:, s, :, :]).then_inc(saved[s], 16)
            for s in range(2):
                sp.wait_ge(saved[s], 16 * (NSUB // 2) + 16)

        @block.vector
        def _(dve):
            v = nc.vector
            dve.wait_ge(iota_in, 16)

            def step(i, b):
                dve.wait_ge(step_done, i + 1)
                v.tensor_tensor(one1[:, b, :, :], iota[:, :].unsqueeze(1).broadcast_to([P, STEP, NK]),
                                e1T[:, bass.ds(i * STEP, STEP)].unsqueeze(2).broadcast_to([P, STEP, NK]),
                                ALU.is_equal).then_inc(dve_hot, 1)
                v.tensor_tensor(raw[:, b, :, :], iota[:, :].unsqueeze(1).broadcast_to([P, SHARED, NK]),
                                e2gT[:, 0, bass.ds(i * STEP + OWN, SHARED)].unsqueeze(2).broadcast_to(
                                    [P, SHARED, NK]), ALU.is_equal).then_inc(raw_done, 1)
                for k in range(OWN):
                    tok = bass.ds(i * STEP + k, 1)
                    gated(v, b, k, e2gT[:, 0, tok], e2gT[:, 1, tok]).then_inc(dve_hot, 1)
            steps(dve, step)

        @block.gpsimd
        def _(pool):
            pool.sem_inc(carried, 1)
            pool.wait_ge(iota_in, 16)

            def step(i, b):
                pool.wait_ge(carried, i + 1)
                pool.wait_ge(few_in, i + 1)
                nc.gpsimd.tensor_tensor(spare[:, :], iota[:, 0:1], iota[:, 0:1], ALU.add).then_inc(carried, 1)
                for k in range(OWN + SHARED, STEP):
                    gated(nc.gpsimd, b, k, few[:, b, 0, k - OWN:k - OWN + 1],
                          few[:, b, 1, k - OWN:k - OWN + 1]).then_inc(pool_hot, 1)
            steps(pool, step)

        @block.tensor
        def _(pe):
            pe.sem_inc(step_done, 2)

            def step(i, b):
                for k in range(STEP):
                    if k % HALF == 0:
                        pe.wait_ge(bank_out, 2 * i + k // HALF + 1)
                    if k < OWN:
                        pe.wait_ge(dve_hot, (OWN + 1) * i + k + 2)
                    elif k < OWN + SHARED:
                        pe.wait_ge(act_hot, SHARED * i + k - OWN + 1)
                    else:
                        pe.wait_ge(pool_hot, (STEP - OWN - SHARED) * i + k - OWN - SHARED + 1)
                    last = nc.tensor.matmul(pg[2 * b + k // HALF][:, (k % HALF) * NK:(k % HALF + 1) * NK],
                                            one2[:, b, k, :], one1[:, b, k, :], start=True, stop=True)
                    if k == HALF - 1:
                        last.then_inc(bank_full, 1)
                last.then_inc(step_done, 1)
            steps(pe, step)

        @block.scalar
        def _(act):
            act.sem_inc(bank_out, 4)

            def few_of(i, b):
                nc.scalar.activation(few[:, b], e2gT[:, :, bass.ds(i * STEP + OWN, STEP - OWN)],
                                     ACT.Copy).then_inc(few_in, 1)
            for i in range(2):
                few_of(i, i)

            def share(i, b):
                act.wait_ge(raw_done, i + 1)
                act.wait_ge(few_in, i + 1)
                for k in range(OWN, OWN + SHARED):
                    nc.scalar.activation(one2[:, b, k, :], raw[:, b, k - OWN, :], ACT.Copy,
                                         scale=few[:, b, 1, k - OWN:k - OWN + 1]).then_inc(act_hot, 1)
            share(0, 0)

            def out(step, parity, b, dst, ahead=True):
                if b == 0:
                    act.wait_ge(bank_full, step + 1)
                else:
                    act.wait_ge(step_done, step + 3)
                    if ahead:
                        few_of(step + 2, parity)
                nc.scalar.activation(dst, pg[2 * parity + b][:, :].rearrange("p (t i) -> p i t", t=HALF),
                                     ACT.Copy).then_inc(bank_out, 1)
            with act.Fori(0, NSUB // 2) as j:
                for s in range(2):
                    act.wait_ge(saved[s], 16 * j + 16)
                    with act.Fori(0, SUB // STEP // 2) as i:
                        for parity in range(2):
                            share((2 * j + s) * (SUB // STEP) + 2 * i + parity + 1, 1 - parity)
                            for b in range(2):
                                out((2 * j + s) * (SUB // STEP) + 2 * i + parity, parity, b,
                                    gbuf[:, s, :, bass.ds((2 * i + parity) * STEP + b * HALF, HALF)])
            for b in range(2):
                out(SEQ // STEP, 0, b, g_tail[:, :, b * HALF:(b + 1) * HALF], ahead=False)


def expert_sweep(nc, A, O, own, sb, ps, sem, ident, hnT, g_dram, g_tail, x2_dram, group,
                 u_raw, v_raw, u_in, v_in, load_rows):
    n0 = f"x{group}_"
    t0 = group * 512
    TG = 512 if group == 0 else T - 512
    CH = -(-TG // 512)
    C = TG // CH
    NV = 4 // CH
    SG = 512 // SUB
    NP = NK // 2
    before = group * NP // 2
    acc = sb(own, n0 + "acc", [P, ND, TG])

    with ExitStack() as st, nc.Block() as block:
        hn_hi, hn_lo = (sb(st, n0 + "hn" + x, [P, ND, TG], F32R) for x in ("h", "l"))
        g_raw = sb(st, n0 + "graw", [P, 2, SG, 2, SUB])
        u_hi, u_lo = (sb(st, n0 + "u" + x, [P, 2, ND, P], F32R) for x in ("h", "l"))
        v_hi, v_lo = (sb(st, n0 + "v" + x, [P, 2, 2, D], F32R) for x in ("h", "l"))
        w_hi, w_lo = (sb(st, n0 + "w" + x, [P, 2, 2, TG], F32R) for x in ("h", "l"))
        gel = sb(st, n0 + "gel", [P, 2, TG])
        wf = sb(st, n0 + "wf", [P, 2, TG])
        pa = [ps(st, f"{n0}pa{i}", (P, CH, 512)) for i in range(2)]
        pv = [ps(st, f"{n0}pv{i}", (P, CH, 512)) for i in range(NV)]
        g_in = [sem(f"x_g_in{i}") for i in range(2)]
        hn_hi_done, hn_lo_done, uhi_done, ulo_done, vhi_done, vlo_done, a_done, gelu_done, wf_done, whi_done, \
            wlo_done, vmm_done, acc_done = (
                sem("x_" + n) for n in ("hnhi", "hnlo", "uhi", "ulo", "vhi", "vlo", "adone", "gelu", "wf", "whi",
                                      "wlo", "vmm", "accd"))

        def steps(eng, body):
            body(0, 0, True, False)
            with eng.Fori(0, NP // 2 - 1) as j:
                body(2 * j + 1, 1, False, False)
                body(2 * j + 2, 0, False, False)
            body(NP - 1, 1, False, True)

        @block.sync
        def _(sp):
            def load_gates(g, s):
                sp.dma_start(g_raw[:, s].rearrange("p c e t -> p c (e t)"),
                             g_dram[group * SG:(group + 1) * SG, :, bass.ds(2 * g, 2), :].rearrange(
                                 "c i e t -> i c (e t)")).then_inc(g_in[s], 16)
            for s in range(2):
                load_gates(s, s)
            with sp.Fori(0, NP // 2 - 1) as j:
                for s in range(2):
                    g = 2 * j + s
                    sp.wait_ge(ulo_done, 2 * g + 2)
                    sp.wait_ge(wf_done, 2 * g + 2)
                    sp.wait_ge(vlo_done, 2 * g + 2)
                    load_rows(sp, g + 2, s)
                    load_gates(g + 2, s)

        @block.tensor
        def _(pe):
            mm = nc.tensor.matmul

            def up(g, e, first):
                n = 2 * g + e
                pe.wait_ge(ulo_done, n + 1)
                for c in range(CH):
                    s = slice(c * C, (c + 1) * C)
                    for k in range(ND):
                        if first and e == 0 and c == 0:
                            pe.wait_ge(hn_lo_done, k + 1)
                        mm(pa[e][:, c, 0:C], u_hi[:, e, k, :], hn_hi[:, k, s], start=(k == 0), stop=False)
                        mm(pa[e][:, c, 0:C], u_hi[:, e, k, :], hn_lo[:, k, s], start=False, stop=False)
                        last = mm(pa[e][:, c, 0:C], u_lo[:, e, k, :], hn_hi[:, k, s], start=False,
                                  stop=(k == ND - 1))
                last.then_inc(a_done, 1)

            def down(g, s):
                pe.wait_ge(wlo_done, 2 * g + 2)
                pe.wait_ge(vlo_done, 2 * g + 2)
                for b in range(ND):
                    pe.wait_ge(acc_done, ND * g + b + 1)
                    d = slice(b * P, (b + 1) * P)
                    for c in range(CH):
                        t = slice(c * C, (c + 1) * C)
                        for e in range(2):
                            mm(pv[b % NV][:, c, 0:C], v_hi[:, s, e, d], w_hi[:, s, e, t], start=(e == 0), stop=False)
                            mm(pv[b % NV][:, c, 0:C], v_hi[:, s, e, d], w_lo[:, s, e, t], start=False, stop=False)
                            last = mm(pv[b % NV][:, c, 0:C], v_lo[:, s, e, d], w_hi[:, s, e, t], start=False,
                                      stop=(e == 1))
                    last.then_inc(vmm_done, 1)

            def body(g, s, first, last):
                for e in range(2):
                    if not first:
                        pe.wait_ge(gelu_done, 2 * g + e - 1)
                    up(g, e, first)
                if not first:
                    down(g - 1, 1 - s)

            pe.sem_inc(vmm_done, 1)
            steps(pe, body)
            down(NP - 1, 1)

        @block.scalar
        def _(act):
            def cp(dst, src):
                return nc.scalar.activation(dst, src, ACT.Copy)

            for k in range(ND):
                cp(hn_hi[:, k, :], hnT[:, k, t0:t0 + TG]).then_inc(hn_hi_done, 1)
                if k == 3 or k == ND - 1:
                    act.wait_ge(u_in[0], 16 * (before + 1))
                    cp(u_hi[:, k // 4], u_raw[:, 0, k // 4]).then_inc(uhi_done, 1)

            def body(g, s, first, last):
                passes = loads_of(g)
                for e in range(2):
                    n = 2 * g + e
                    act.wait_ge(a_done, n + 1)
                    if not first:
                        act.wait_ge(wf_done, n - 1)
                    nc.scalar.activation(gel[:, e, :].rearrange("p (c t) -> p c t", c=CH), pa[e][:, :, 0:C],
                                         ACT.Gelu).then_inc(gelu_done, 1)
                    if not last:
                        act.wait_ge(u_in[1 - s], 16 * (before + loads_of(g + 1)))
                        cp(u_hi[:, e], u_raw[:, 1 - s, e]).then_inc(uhi_done, 1)
                    if e == 0 and not first:
                        act.wait_ge(vmm_done, ND * (g - 1) + 1)
                    act.wait_ge(v_in[s], 16 * (before + passes))
                    cp(v_hi[:, s, e, :], v_raw[:, s, e, :]).then_inc(vhi_done, 1)
                    act.wait_ge(wf_done, n + 1)
                    cp(w_hi[:, s, e, :], wf[:, e, :]).then_inc(whi_done, 1)
            steps(act, body)

        @block.vector
        def _(dve):
            v = nc.vector

            def lo(dst, src, hi):
                return v.tensor_tensor(dst, src, hi.bitcast(F32), ALU.subtract)

            for k in range(ND):
                dve.wait_ge(hn_hi_done, k + 1)
                lo(hn_lo[:, k, :], hnT[:, k, t0:t0 + TG], hn_hi[:, k, :]).then_inc(hn_lo_done, 1)
                if k == 3 or k == ND - 1:
                    e = k // 4
                    dve.wait_ge(uhi_done, e + 1)
                    lo(u_lo[:, e], u_raw[:, 0, e], u_hi[:, e]).then_inc(ulo_done, 1)
            v.memset(acc[:, :, :], 0.0).then_inc(acc_done, NV)

            def add(g, blocks):
                for b in blocks:
                    if b == 0:
                        dve.wait_ge(acc_done, NV + ND * g)
                    dve.wait_ge(vmm_done, ND * g + b + 2)
                    a3 = acc[:, b, :].rearrange("p (c t) -> p c t", c=CH)
                    v.tensor_tensor(a3, a3, pv[b % NV][:, :, 0:C], ALU.add).then_inc(acc_done, 1)

            def body(g, s, first, last):
                passes = loads_of(g)

                def sums(e, part):
                    if e == 1 and not first:
                        add(g - 1, (2 * part, 2 * part + 1))

                for e in range(2):
                    n = 2 * g + e
                    sums(e, 0)
                    if not last:
                        dve.wait_ge(uhi_done, n + 3)
                        lo(u_lo[:, e], u_raw[:, 1 - s, e], u_hi[:, e]).then_inc(ulo_done, 1)
                    sums(e, 1)
                    dve.wait_ge(gelu_done, n + 1)
                    dve.wait_ge(g_in[s], 16 * passes)
                    if not first:
                        dve.wait_ge(whi_done, n - 1)
                        dve.wait_ge(wlo_done, n - 1)
                    mul = v.tensor_tensor(wf[:, e, 0:512].rearrange("p (c t) -> p c t", c=SG),
                                          gel[:, e, 0:512].rearrange("p (c t) -> p c t", c=SG), g_raw[:, s, :, e, :],
                                          ALU.mult)
                    if group:
                        mul = v.tensor_tensor(wf[:, e, 512:TG], gel[:, e, 512:TG], g_tail[:, n, :], ALU.mult)
                    mul.then_inc(wf_done, 1)
                    sums(e, 2)
                    dve.wait_ge(vhi_done, n + 1)
                    lo(v_lo[:, s, e, :], v_raw[:, s, e, :], v_hi[:, s, e, :]).then_inc(vlo_done, 1)
                    sums(e, 3)
                    dve.wait_ge(whi_done, n + 1)
                    lo(w_lo[:, s, e, :], wf[:, e, :], w_hi[:, s, e, :]).then_inc(wlo_done, 1)
            steps(dve, body)
            add(NP - 1, range(ND))

    TL = range(4) if group == 0 else range(4, NT)
    with ExitStack() as st, nc.Block() as block:
        x2 = sb(st, n0 + "x2", [P, NT, D])
        gf = sb(st, n0 + "gf", [P, D])
        junk = sb(st, n0 + "junk", [P, D])
        ss = sb(st, n0 + "ss", [P, NT])
        rstd = sb(st, n0 + "rstd", [P, NT])
        pt = [ps(st, f"{n0}pt{i}") for i in range(4)]
        x_in = [sem(f"x_e_xin{i}") for i in range(5)]
        g_in2, ones_set, tr_done, x_done, sq_done, ms_done, root_done, rstd_done, y_done, y_out = (
            sem("x_e_" + n) for n in ("g", "ones", "tr", "x", "sq", "ms", "root", "rstd", "y", "out"))

        @block.sync
        def _(sp):
            sp.dma_start(gf[:, :], A["g_final"]).then_inc(g_in2, 16)
            for t in TL:
                sp.dma_start(x2[:rows(t), t, :], x2_dram[t * P:t * P + rows(t), :]).then_inc(x_in[t - TL[0]], 16)
            if group == 0:
                load_rows(sp, 0, 0)
            for i, t in enumerate(TL):
                sp.wait_ge(y_done, i + 1)
                sp.dma_start(O["y"][t * P:t * P + rows(t), :], x2[:rows(t), t, :]).then_inc(y_out, 16)
            if group == 0:
                load_rows(sp, 1, 1)
            sp.wait_ge(y_out, 16 * len(TL))

        @block.tensor
        def _(pe):
            for i, t in enumerate(TL):
                for n in range(2):
                    u = 2 * i + n
                    if u >= 4:
                        pe.wait_ge(x_done, u - 3)
                    for k in range(4):
                        last = nc.tensor.transpose(pt[u % 4][:rows(t), k * P:(k + 1) * P],
                                                   acc[:, 4 * n + k, t * P - t0:t * P - t0 + rows(t)], ident[:, :])
                    last.then_inc(tr_done, 1)

        @block.scalar
        def _(act):
            act.wait_ge(ones_set, 1)
            for i, t in enumerate(TL):
                act.wait_ge(x_done, 2 * i + 2)
                if i:
                    act.wait_ge(sq_done, i)
                nc.scalar.activation(junk[:rows(t), :], x2[:rows(t), t, :], ACT.Square,
                                     accum_out=ss[:rows(t), t:t + 1]).then_inc(sq_done, 1)
            act.wait_ge(ms_done, 1)
            nc.scalar.activation(rstd[:, :], ss[:, :], ACT.Sqrt).then_inc(root_done, 1)

        @block.vector
        def _(dve):
            nc.vector.memset(ss[:, :], 1.0).then_inc(ones_set, 1)
            for i, t in enumerate(TL):
                dve.wait_ge(x_in[i], 16)
                for n in range(2):
                    u = 2 * i + n
                    s = slice(n * 512, (n + 1) * 512)
                    dve.wait_ge(tr_done, u + 1)
                    nc.vector.tensor_tensor(x2[:rows(t), t, s], pt[u % 4][:rows(t), :], x2[:rows(t), t, s],
                                            ALU.add).then_inc(x_done, 1)
            dve.wait_ge(sq_done, len(TL))
            nc.vector.tensor_scalar(ss[:, :], ss[:, :], 1.0 / D, EPS, ALU.mult, ALU.add).then_inc(ms_done, 1)
            dve.wait_ge(root_done, 1)
            nc.vector.reciprocal(rstd[:, :], rstd[:, :]).then_inc(rstd_done, 1)
            dve.wait_ge(rstd_done, 1)
            dve.wait_ge(g_in2, 16)
            for i, t in enumerate(TL):
                nc.vector.scalar_tensor_tensor(x2[:rows(t), t, :], x2[:rows(t), t, :], rstd[:rows(t), t:t + 1],
                                               gf[:rows(t), :], ALU.mult, ALU.mult).then_inc(y_done, 1)


def loads_of(g):
    return g // 2 + 1


def constants():
    f = np.float32
    j, t = np.arange(P)[:, None], np.arange(P)[None, :]
    lg = np.log1p(-np.power(2.0, -5.0 - np.arange(H)))
    dmat = np.stack([np.where(j <= t, np.exp(np.maximum(t - j, 0) * g), 0.0) for g in lg], axis=1)
    idx = np.arange(P)[:, None]
    rcol = np.stack([np.exp((idx + 1) * lg), np.exp((P - 1 - idx) * lg), np.exp(P * lg) + 0 * idx], axis=1)
    inv = np.power(f(10000.0), -np.arange(P // 2, dtype=f) * f(2.0 / P)).astype(f)
    ang = (np.arange(SEQ, dtype=f)[:, None] * inv).astype(f).astype(np.float64)
    cosin = np.stack([np.cos(ang), np.sin(ang)]).reshape(2, NC, P, P // 2).transpose(2, 0, 1, 3)
    start = np.ones((H, T))
    start[:, 0:SEQ:P] = 0
    start[:, SEQ:] = 0
    c = {
        "ident": np.eye(P),
        "iota": np.broadcast_to(np.arange(P), (P, P)),
        "start_mask": start,
        "delta4": np.eye(H),
        "ones4": np.ones((H, P)),
        "neg": np.where(j <= t, 0.0, NEG),
        "dmask": np.broadcast_to((np.eye(NS) * SCALE)[:, :, None], (NS, NS, P)),
        "dmat": dmat,
        "cosin": cosin,
        "rcol": rcol,
        "rdec1": np.broadcast_to(np.exp(lg), (P, H)),
        "inv": np.broadcast_to(inv, (NS, P // 2)),
    }
    return {k: np.ascontiguousarray(v, dtype=f) for k, v in c.items()}


def lay_out(x_prompt, x_sample, state_mlstm_C, state_mlstm_n, state_mlstm_m, state_ret_S, pos_sample,
            rms_mix_g, w_in, b_igate, b_fgate, norm_mlstm_g, norm_ret_g, w_out, rms_ffn_g,
            w_query, sub_keys, peer_u, peer_v, rms_final_g):
    def by_block(m):
        return m.reshape(-1, P, m.shape[-1]).transpose(1, 0, 2)

    w = w_in[0]
    HP = H * P
    off_i, off_r = 4 * HP, 4 * HP + 2 * H
    heads = [by_block(np.concatenate([w[:, o + s * HP + h * P:o + s * HP + (h + 1) * P] for s in range(4)], axis=1))
             for o in (0, off_r) for h in range(H)]
    gains = np.stack([g.reshape(ND, P).T for g in (rms_mix_g[0], np.concatenate([norm_mlstm_g[0], norm_ret_g[0]]),
                                                   rms_ffn_g[0], rms_final_g)], axis=1)
    cn = np.concatenate([state_mlstm_C[0], state_mlstm_n[0][..., None]], axis=-1)
    return {
        "x": np.concatenate([x_prompt[0], x_sample[:, 0]]),
        "gains": gains,
        "w_heads": np.stack(heads),
        "w_if": by_block(w[:, off_i:off_r]),
        "b_if": np.stack([b_igate[0], b_fgate[0]], axis=1),
        "m_in": state_mlstm_m[0].T,
        "csm": cn.transpose(2, 1, 0, 3),
        "csr": state_ret_S[0].transpose(2, 1, 0, 3),
        "pos": pos_sample.reshape(NS, 1),
        "w_out": by_block(w_out[0]),
        "w_query": by_block(w_query[0]).reshape(P, ND, PH, 2 * P).transpose(2, 0, 1, 3),
        "sub_keys": sub_keys[0].transpose(3, 0, 1, 2),
        "peer_u": peer_u[0].reshape(NK // 2, 2, P, ND, P).transpose(0, 4, 1, 3, 2),
        "peer_v": peer_v[0].reshape(NK // 2, 2, P, D).transpose(0, 2, 1, 3),
        "g_final": np.broadcast_to(rms_final_g, (P, D)),
    }


OUTPUTS = {"y": (T, D), "cm": (H, P, P + 1), "csm": (H, P, NS, P + 1), "m": (H, 1 + NS), "cr": (H, P, P), "csr": (H, P, NS, P)}


def kernel(**inputs):
    import concourse.bacc as bacc
    from concourse.bass_utils import run_bass_kernel_spmd

    nc = bacc.Bacc("TRN2", target_bir_lowering=False, num_devices=1)
    arrays = {**lay_out(**{k: np.asarray(v) for k, v in inputs.items()}), **constants()}
    arrays = {f"in_{k}": np.ascontiguousarray(v) for k, v in arrays.items()}
    A = {k[3:]: nc.dram_tensor(k, v.shape, mybir.dt.from_np(v.dtype), kind="ExternalInput").ap()
         for k, v in arrays.items()}
    O = {k: nc.dram_tensor(f"out_{k}", s, F32, kind="ExternalOutput").ap() for k, s in OUTPUTS.items()}
    build(nc, A, O)
    got = run_bass_kernel_spmd(nc, [arrays], core_ids=[0]).results[0]
    y, cm, csm, m, cr, csr = (np.asarray(got[f"out_{k}"]) for k in ("y", "cm", "csm", "m", "cr", "csr"))
    csm = csm.transpose(2, 0, 1, 3)
    out = (y[None, :SEQ], y[SEQ:, None], cm[None, None, ..., :P], cm[None, None, ..., P], m[:, 0].reshape(1, 1, H),
           cr[None, None], csm[None, ..., :P], csm[None, ..., P], m[:, 1:].T[None], csr.transpose(2, 0, 1, 3)[None])
    return tuple(np.ascontiguousarray(o) for o in out)
```
